# Optimizing a Trainium2 kernel written in Bass

```python
import math
import jax, jax.numpy as jnp
from jax import lax
import numpy as np

D_MODEL = 1024
BATCH = 1
SEQ = 512
DEPTH = 2

GRID_W = 64
CTX_LEN = 256
N_MIXERS = 2
N_SSD_LAYERS = (DEPTH + 1) // 2
N_ATTN_LAYERS = DEPTH // 2
EPS = 1e-6

SSD_EXPAND = 2
SSD_D_INNER = SSD_EXPAND * D_MODEL
SSD_HEADDIM = 64
SSD_HEADS = SSD_D_INNER // SSD_HEADDIM
SSD_GROUPS = 4
SSD_HPG = SSD_HEADS // SSD_GROUPS
SSD_STATE = 128
SSD_CONV_W = 5
SSD_CHUNK = 128
SSD_CONV_DIM = SSD_D_INNER + 2 * SSD_GROUPS * SSD_STATE
SSD_IN_DIM = SSD_D_INNER + SSD_CONV_DIM + 2 * SSD_HEADS

DA_HEADS = 8
DA_HEAD_DIM = 64
DA_QK_DIM = 2 * DA_HEADS * DA_HEAD_DIM
DA_V_DIM = DA_HEADS * 2 * DA_HEAD_DIM
Q_BLOCK = 128
ROPE_BASE = 10000.0

PEER_HEADS = 8
PEER_NKEYS = 128
PEER_EXPERTS = PEER_NKEYS ** 2
PEER_DKEY = 256
PEER_TOPK = 16
PEER_BLOCK = 128

kernel_name = 'hybrid_ssd_diffattn_peer_dit'

def rmsnorm(x, g):
    xf = x.astype(jnp.float32)
    y = xf * lax.rsqrt(jnp.mean(xf * xf, axis=-1, keepdims=True) + EPS)
    return (y * g.astype(jnp.float32)).astype(x.dtype)

def modulate(x, g, shift, scale):
    return rmsnorm(x, g) * (1.0 + scale) + shift

def ada_mod(cvec, w, b):
    m = jax.nn.silu(cvec) @ w + b
    return jnp.split(m[..., None, :], 6, axis=-1)

def flip(t):
    return jnp.flip(t, axis=1)

def axial_rope_tables(length):
    rows = length // GRID_W
    row = jnp.repeat(jnp.arange(rows, dtype=jnp.float32), GRID_W)
    col = jnp.tile(jnp.arange(GRID_W, dtype=jnp.float32), rows)
    half = DA_HEAD_DIM // 2
    freqs = ROPE_BASE ** (-jnp.arange(0, half, 2, dtype=jnp.float32) / half)
    ang_r = row[:, None] * freqs
    ang_c = col[:, None] * freqs
    ang = jnp.concatenate([ang_r, ang_r, ang_c, ang_c], axis=-1)
    return jnp.cos(ang), jnp.sin(ang)

def rotate_half_axial(x):
    x1, x2, x3, x4 = jnp.split(x, 4, axis=-1)
    return jnp.concatenate([-x2, x1, -x4, x3], axis=-1)

def apply_rope(x, cos, sin):
    return x * cos.astype(x.dtype) + rotate_half_axial(x) * sin.astype(x.dtype)

def centred_dwconv(x, w, b):
    pad = SSD_CONV_W // 2
    length = x.shape[1]
    xp = jnp.pad(x, ((0, 0), (pad, pad), (0, 0)))
    y = b + sum(xp[:, k:k + length] * w[k] for k in range(SSD_CONV_W))
    return jax.nn.silu(y)

def ssd_chunk_scan(xs, dt, a, bm, cm, d, h0):
    bsz, length = xs.shape[:2]
    nc = length // SSD_CHUNK

    def chunks(t):
        return jnp.moveaxis(t.reshape(bsz, nc, SSD_CHUNK, *t.shape[2:]), 1, 0)

    lower = jnp.tril(jnp.ones((SSD_CHUNK, SSD_CHUNK), dtype=bool))[None, :, :, None, None]

    def step(h, inp):
        xc, dtc, bc, cc = inp
        dtc = dtc.astype(jnp.float32)
        xf = xc.astype(jnp.float32)
        bf = bc.astype(jnp.float32)
        cf = cc.astype(jnp.float32)
        cs = jnp.cumsum(dtc * a, axis=1)
        seg = cs[:, :, None] - cs[:, None, :]
        decay = jnp.exp(jnp.where(lower, seg, -jnp.inf))
        cb = jnp.einsum('bign,bjgn->bijg', cf, bf)
        w = cb[..., None] * decay * dtc[:, None]
        y = jnp.einsum('bijgr,bjgrp->bigrp', w, xf)
        y = y + jnp.einsum('bign,bgrpn->bigrp', cf, h) * jnp.exp(cs)[..., None]
        y = y + d[..., None].astype(jnp.float32) * xf
        w_end = jnp.exp(cs[:, -1:] - cs) * dtc
        h = jnp.exp(cs[:, -1])[..., None, None] * h + jnp.einsum('bjgr,bjgn,bjgrp->bgrpn', w_end, bf, xf)
        return h, y.astype(xc.dtype)

    h_final, ys = lax.scan(step, h0, (chunks(xs), chunks(dt), chunks(bm), chunks(cm)))
    return jnp.moveaxis(ys, 0, 1).reshape(xs.shape), h_final

def ssd_project(h, in_w, conv_w, conv_b, dt_bias):
    bsz, length, _ = h.shape
    zxbcdt = h @ in_w
    z = zxbcdt[..., :SSD_D_INNER]
    xbc = centred_dwconv(zxbcdt[..., SSD_D_INNER:SSD_D_INNER + SSD_CONV_DIM], conv_w, conv_b)
    dt = zxbcdt[..., SSD_D_INNER + SSD_CONV_DIM:].reshape(bsz, length, 2, SSD_HEADS)
    dt = jax.nn.softplus(dt.astype(jnp.float32) + dt_bias.astype(jnp.float32))
    dt = dt.reshape(bsz, length, 2, SSD_GROUPS, SSD_HPG)
    gn = SSD_GROUPS * SSD_STATE
    xs = xbc[..., :SSD_D_INNER].reshape(bsz, length, SSD_GROUPS, SSD_HPG, SSD_HEADDIM)
    bm = xbc[..., SSD_D_INNER:SSD_D_INNER + gn].reshape(bsz, length, SSD_GROUPS, SSD_STATE)
    cm = xbc[..., SSD_D_INNER + gn:].reshape(bsz, length, SSD_GROUPS, SSD_STATE)
    return z, xs, dt, bm, cm

def ssd_layer(h_lat, h_ctx, in_w, conv_w, conv_b, dt_bias, a_log, d_skip, norm_g, out_w):
    a = -jnp.exp(a_log.astype(jnp.float32)).reshape(2, SSD_GROUPS, SSD_HPG)
    d = d_skip.reshape(2, SSD_GROUPS, SSD_HPG)

    def mix(h, h0_f, h0_b):
        z, xs, dt, bm, cm = ssd_project(h, in_w, conv_w, conv_b, dt_bias)
        y_f, h_f = ssd_chunk_scan(xs, dt[:, :, 0], a[0], bm, cm, d[0], h0_f)
        y_b, h_b = ssd_chunk_scan(flip(xs), flip(dt[:, :, 1]), a[1], flip(bm), flip(cm), d[1], h0_b)
        y = (y_f + flip(y_b)).reshape(h.shape[0], h.shape[1], SSD_D_INNER)
        return rmsnorm(y * jax.nn.silu(z), norm_g) @ out_w, h_f, h_b

    h0 = jnp.zeros((h_ctx.shape[0], SSD_GROUPS, SSD_HPG, SSD_HEADDIM, SSD_STATE), jnp.float32)
    y_ctx, hc_f, hc_b = mix(h_ctx, h0, h0)
    y_lat, _, _ = mix(h_lat, hc_f, hc_b)
    return y_lat, y_ctx

def diff_attend(q, k, v, lam):
    s = jnp.einsum('mbhqd,mbhkd->mbhqk', q, k).astype(jnp.float32)
    p = jax.nn.softmax(s, axis=-1)
    w = p[0] - lam * p[1]
    return jnp.einsum('bhqk,bhkv->bhqv', w.astype(v.dtype), v)

def diff_attention_layer(h_lat, h_ctx, qkv_w, lam_q, lam_k, subln_g, out_w, lambda_init, cos, sin, ctx_out):
    lam = (jnp.exp(jnp.sum(lam_q[0] * lam_k[0]).astype(jnp.float32))
           - jnp.exp(jnp.sum(lam_q[1] * lam_k[1]).astype(jnp.float32)) + lambda_init)

    def project(h):
        bsz, length, _ = h.shape
        q, k, v = jnp.split(h @ qkv_w, [DA_QK_DIM, 2 * DA_QK_DIM], axis=-1)
        q = q.reshape(bsz, length, 2, DA_HEADS, DA_HEAD_DIM).transpose(2, 0, 3, 1, 4) * DA_HEAD_DIM ** -0.5
        k = k.reshape(bsz, length, 2, DA_HEADS, DA_HEAD_DIM).transpose(2, 0, 3, 1, 4)
        v = v.reshape(bsz, length, DA_HEADS, 2 * DA_HEAD_DIM).transpose(0, 2, 1, 3)
        return q, k, v

    def merge_heads(o):
        bsz, _, length, _ = o.shape
        o = rmsnorm(o, subln_g) * (1.0 - lambda_init)
        return o.transpose(0, 2, 1, 3).reshape(bsz, length, DA_V_DIM) @ out_w

    q_c, k_c, v_c = project(h_ctx)
    q_l, k_l, v_l = project(h_lat)
    q_l = apply_rope(q_l, cos, sin)
    k_l = apply_rope(k_l, cos, sin)
    k_all = jnp.concatenate([k_c, k_l], axis=3)
    v_all = jnp.concatenate([v_c, v_l], axis=2)
    bsz, length = h_lat.shape[:2]
    nb = length // Q_BLOCK
    q_blocks = jnp.moveaxis(q_l.reshape(2, bsz, DA_HEADS, nb, Q_BLOCK, DA_HEAD_DIM), 3, 0)
    o_blocks = lax.map(lambda qb: diff_attend(qb, k_all, v_all, lam), q_blocks)
    o_lat = jnp.moveaxis(o_blocks, 0, 2).reshape(bsz, DA_HEADS, length, 2 * DA_HEAD_DIM)
    y_lat = merge_heads(o_lat)
    y_ctx = merge_heads(diff_attend(q_c, k_c, v_c, lam)) if ctx_out else None
    return y_lat, y_ctx

def peer_ffn(h, w_q, sub_keys, u_tab, v_tab):
    bsz, length, _ = h.shape
    q = (h @ w_q).reshape(bsz, length, PEER_HEADS, 2, PEER_DKEY // 2)
    s = jnp.einsum('blhcd,hcnd->blhcn', q, sub_keys).astype(jnp.float32)
    s_top, i_top = lax.top_k(s, PEER_TOPK)
    kk = PEER_TOPK * PEER_TOPK
    cand_s = (s_top[..., 0, :, None] + s_top[..., 1, None, :]).reshape(bsz, length, PEER_HEADS, kk)
    cand_i = (i_top[..., 0, :, None] * PEER_NKEYS + i_top[..., 1, None, :]).reshape(bsz, length, PEER_HEADS, kk)
    best_s, best_pos = lax.top_k(cand_s, PEER_TOPK)
    best_i = jnp.take_along_axis(cand_i, best_pos, axis=-1)
    gate = jax.nn.softmax(best_s, axis=-1)
    ids = best_i.reshape(bsz, length, PEER_HEADS * PEER_TOPK)
    gate = gate.reshape(bsz, length, PEER_HEADS * PEER_TOPK).astype(h.dtype)
    nb = length // PEER_BLOCK

    def blocks(t):
        return jnp.moveaxis(t.reshape(bsz, nb, PEER_BLOCK, *t.shape[2:]), 1, 0)

    def expert_block(args):
        hb, ib, gb = args
        act = jax.nn.gelu(jnp.einsum('btd,bted->bte', hb, u_tab[ib]), approximate=False)
        return jnp.einsum('bte,bted->btd', gb * act, v_tab[ib])

    out = lax.map(expert_block, (blocks(h), blocks(ids), blocks(gate)))
    return jnp.moveaxis(out, 0, 1).reshape(bsz, length, D_MODEL)

def setup_inputs(seed: int = 0) -> dict:
    key = jax.random.key(seed)
    ks = jax.random.split(key, 32)
    f32 = jnp.float32
    D = D_MODEL

    def nrm(k, shape, s):
        return jax.random.normal(k, shape, f32) * s

    dt0 = jnp.exp(jax.random.uniform(ks[11], (N_SSD_LAYERS, 2, SSD_HEADS), f32, math.log(1e-3), math.log(1e-1)))
    return {
        'x': nrm(ks[0], (BATCH, SEQ, D), 1.0),
        'c': nrm(ks[1], (BATCH, D), 1.0),
        'ctx': nrm(ks[2], (BATCH, CTX_LEN, D), 1.0),
        'c_ctx': nrm(ks[3], (D,), 1.0),
        'ada_w': nrm(ks[4], (DEPTH, D, 6 * D), 0.5 * D ** -0.5),
        'ada_b': nrm(ks[5], (DEPTH, 6 * D), 0.02),
        'norm_mix_g': 1.0 + nrm(ks[6], (DEPTH, D), 0.02),
        'norm_ffn_g': 1.0 + nrm(ks[7], (DEPTH, D), 0.02),
        'ssd_in_w': nrm(ks[8], (N_SSD_LAYERS, D, SSD_IN_DIM), D ** -0.5),
        'ssd_conv_w': nrm(ks[9], (N_SSD_LAYERS, SSD_CONV_W, SSD_CONV_DIM), SSD_CONV_W ** -0.5),
        'ssd_conv_b': nrm(ks[10], (N_SSD_LAYERS, SSD_CONV_DIM), 0.02),
        'ssd_dt_bias': dt0 + jnp.log(-jnp.expm1(-dt0)),
        'ssd_a_log': jnp.log(jax.random.uniform(ks[12], (N_SSD_LAYERS, 2, SSD_HEADS), f32, 1.0, 16.0)),
        'ssd_d': 1.0 + nrm(ks[13], (N_SSD_LAYERS, 2, SSD_HEADS), 0.1),
        'ssd_norm_g': 1.0 + nrm(ks[14], (N_SSD_LAYERS, SSD_D_INNER), 0.02),
        'ssd_out_w': nrm(ks[15], (N_SSD_LAYERS, SSD_D_INNER, D), SSD_D_INNER ** -0.5),
        'attn_qkv_w': nrm(ks[16], (N_ATTN_LAYERS, D, 2 * DA_QK_DIM + DA_V_DIM), D ** -0.5),
        'attn_lambda_q': nrm(ks[17], (N_ATTN_LAYERS, 2, DA_HEAD_DIM), 0.1),
        'attn_lambda_k': nrm(ks[18], (N_ATTN_LAYERS, 2, DA_HEAD_DIM), 0.1),
        'attn_subln_g': 1.0 + nrm(ks[19], (N_ATTN_LAYERS, 2 * DA_HEAD_DIM), 0.02),
        'attn_out_w': nrm(ks[20], (N_ATTN_LAYERS, DA_V_DIM, D), DA_V_DIM ** -0.5),
        'peer_q_w': nrm(ks[21], (DEPTH, D, PEER_HEADS * PEER_DKEY), D ** -0.5),
        'peer_keys': nrm(ks[22], (DEPTH, PEER_HEADS, 2, PEER_NKEYS, PEER_DKEY // 2), (PEER_DKEY // 2) ** -0.5),
        'peer_u': nrm(ks[23], (DEPTH, PEER_EXPERTS, D), D ** -0.5),
        'peer_v': nrm(ks[24], (DEPTH, PEER_EXPERTS, D), 0.5),
        'final_norm_g': 1.0 + nrm(ks[25], (D,), 0.02),
    }

def reference(x, c, ctx, c_ctx, ada_w, ada_b, norm_mix_g, norm_ffn_g, ssd_in_w, ssd_conv_w, ssd_conv_b,
              ssd_dt_bias, ssd_a_log, ssd_d, ssd_norm_g, ssd_out_w, attn_qkv_w, attn_lambda_q, attn_lambda_k,
              attn_subln_g, attn_out_w, peer_q_w, peer_keys, peer_u, peer_v, final_norm_g):
    cos, sin = axial_rope_tables(x.shape[1])
    for i in range(DEPTH):
        last = i == DEPTH - 1
        sh1, sc1, g1, sh2, sc2, g2 = ada_mod(c, ada_w[i], ada_b[i])
        csh1, csc1, cg1, csh2, csc2, cg2 = ada_mod(c_ctx, ada_w[i], ada_b[i])
        h = modulate(x, norm_mix_g[i], sh1, sc1)
        hc = modulate(ctx, norm_mix_g[i], csh1, csc1)
        j = i // N_MIXERS
        if i % N_MIXERS == 0:
            y, yc = ssd_layer(h, hc, ssd_in_w[j], ssd_conv_w[j], ssd_conv_b[j], ssd_dt_bias[j],
                              ssd_a_log[j], ssd_d[j], ssd_norm_g[j], ssd_out_w[j])
        else:
            lambda_init = 0.8 - 0.6 * math.exp(-0.3 * i)
            y, yc = diff_attention_layer(h, hc, attn_qkv_w[j], attn_lambda_q[j], attn_lambda_k[j],
                                         attn_subln_g[j], attn_out_w[j], lambda_init, cos, sin, not last)
        x = x + g1 * y
        x = x + g2 * peer_ffn(modulate(x, norm_ffn_g[i], sh2, sc2), peer_q_w[i], peer_keys[i], peer_u[i], peer_v[i])
        if not last:
            ctx = ctx + cg1 * yc
            ctx = ctx + cg2 * peer_ffn(modulate(ctx, norm_ffn_g[i], csh2, csc2),
                                       peer_q_w[i], peer_keys[i], peer_u[i], peer_v[i])
    return rmsnorm(x, final_norm_g)


_drawn_inputs = setup_inputs


def setup_inputs(seed=0):
    import zlib

    import numpy as np

    out = dict(_drawn_inputs(seed))
    spreads = {}
    factors = {'norm_mix_g': 3.901,
     'norm_ffn_g': 3.252,
     'ssd_conv_b': 4.152,
     'ssd_d': 16.806,
     'ssd_norm_g': 4.832,
     'attn_lambda_q': 6.407,
     'attn_lambda_k': 7.597,
     'attn_subln_g': 30.114,
     'final_norm_g': 7.924}
    for name, (base, spread) in spreads.items():
        noise = np.random.default_rng([zlib.crc32(name.encode()), seed]).standard_normal(out[name].shape)
        drawn = base * np.exp(spread * noise) if base else spread * noise
        out[name] = __import__('jax').numpy.asarray(drawn.astype(out[name].dtype))
    for name, factor in factors.items():
        out[name] = (out[name] * factor).astype(out[name].dtype)
    return out
```

```python
from contextlib import ExitStack
import math

import numpy as np
import concourse.bass as bass
from concourse import mybir

ALU = mybir.AluOpType
ACT = mybir.ActivationFunctionType
AX = mybir.AxisListType
F32 = mybir.dt.float32
U32 = mybir.dt.uint32

P = 128
D = 1024
KD = D // P
LAT, CTX = 4, 2
NT = LAT + CTX
T = NT * P
TL = LAT * P
EPS = 1e-6
BANK = 512

DI = 2048
MX, MB = DI // P, 4
HEADS, GROUPS, HPG, HD = 32, 4, 8, 64
DH = 2 * HEADS

AH, AV = 8, 128
LAMBDA_INIT = 0.8 - 0.6 * math.exp(-0.3)

PH, TOPK, NKEYS = 8, 16, 128
HC = 2 * PH
SLOTS = 8
NEG = -3.0e38


def bcast(ap, shape):
    return ap.broadcast_to(shape)


class Core:

    def __init__(self, nc, ctx, ins, debug):
        self.nc, self.ctx, self.ins = nc, ctx, ins
        self.names, self.stage_sems = {}, []
        self.ps = ctx.enter_context(nc.psum_tensor("ps", [P, 8, BANK], F32))
        self.flat = self.ps[:].rearrange("p b n -> p (b n)")
        kind = "ExternalOutput" if debug else "Internal"
        scratch = lambda name, shape: nc.dram_tensor(name, shape, F32, kind=kind).ap()
        self.mods = scratch("mods", [2, NT, 6 * D])
        self.h = scratch("h_scratch", [NT, P, D])
        self.z = scratch("z_scratch", [4, NT, P, BANK])
        self.xs = [scratch(f"x_scratch{i}", [NT, P, D]) for i in range(4)]
        self.passed = {e: self.sem(f"{e}_passed") for e in ("pe", "dve", "act", "pool", "sp")}
        self.stage_sems = []

    def sem(self, name):
        n = self.names[name] = self.names.get(name, -1) + 1
        handle = self.nc.alloc_semaphore(name=f"{name}_{n}")
        self.stage_sems.append(handle)
        return handle

    def end_stage(self):
        self.nc.clear_and_free_semaphores(self.stage_sems)
        self.nc.all_engine_barrier()
        self.stage_sems = []

    def hold(self, engine, who, sem, value):
        engine.wait_ge(sem, value)
        engine.sem_inc(self.passed[who], 1)


def sbuf(ctx, nc):
    def allocate(name, shape, dt=F32):
        return ctx.enter_context(nc.sbuf_tensor(f"{name}_{nc.next_id()}", shape, dt))
    return allocate


def modulation_stage(k):
    nc, ins = k.nc, k.ins
    CH, RING = 12, 3
    with ExitStack() as ctx:
        sb = sbuf(ctx, nc)
        c = sb("ada_c", [P, KD, 2])
        cs = sb("ada_silu", [P, KD, 2])
        w = sb("ada_w", [P, RING, KD * BANK])
        bias = sb("ada_bias", [2, 2 * 6 * D])
        m = sb("ada_m", [2, 2 * 6 * D])
        c_in, b_in, silu = k.sem("c_in"), k.sem("b_in"), k.sem("silu")
        w_in = [k.sem(f"ada_w_in{s}") for s in range(RING)]
        w_free, ps_full, ps_free = k.sem("ada_w_free"), k.sem("ada_ps_full"), k.sem("ada_ps_free")
        done = k.sem("ada_done")
        block = ctx.enter_context(nc.Block())

        @block.sync
        def _(sp):
            sp.dma_start(c[:], ins["c_cols"]).then_inc(c_in, 16)
            for r in range(2):
                sp.dma_start(bias[r:r + 1, :], ins["ada_b"]).then_inc(b_in, 16)
            with sp.Fori(0, 2 * CH // RING) as i:
                for s in range(RING):
                    sp.wait_ge(w_free, i * RING + s + 1)
                    sp.dma_start(w[:, s, :], ins["ada_w"][bass.ds(i * RING + s, 1)].rearrange(
                        "o p n -> (o p) n")).then_inc(w_in[s], 16)
            sp.wait_ge(ps_free, RING + 2 * CH)
            for l in range(2):
                for t in range(NT):
                    r = 0 if t < LAT else 1
                    sp.dma_start(k.mods[l, t:t + 1, :], m[r:r + 1, l * 6 * D:(l + 1) * 6 * D]).then_inc(done, 16)
            sp.wait_ge(done, 16 * 2 * NT)

        @block.scalar
        def _(act):
            act.wait_ge(c_in, 16)
            nc.scalar.activation(cs[:], c[:], ACT.Silu).then_inc(silu, 1)

        @block.tensor
        def _(pe):
            pe.sem_inc(w_free, RING)
            pe.wait_ge(silu, 1)
            with pe.Fori(0, 2 * CH // RING) as i:
                for s in range(RING):
                    pe.wait_ge(w_in[s], (i + 1) * 16)
                    k.hold(pe, "pe", ps_free, i * RING + s + 1)
                    for kt in range(KD):
                        mm = nc.tensor.matmul(k.ps[0:2, s, :], cs[:, kt, :], w[:, s, kt * BANK:(kt + 1) * BANK],
                                              start=kt == 0, stop=kt == KD - 1)
                    mm.then_inc(ps_full, 1)

        @block.vector
        def _(dve):
            dve.sem_inc(ps_free, RING)
            dve.wait_ge(b_in, 32)
            with dve.Fori(0, 2 * CH // RING) as i:
                for s in range(RING):
                    k.hold(dve, "dve", ps_full, i * RING + s + 1)
                    at = bass.ds((i * RING + s) * BANK, BANK)
                    nc.vector.tensor_tensor(m[:, at], k.ps[0:2, s, :], bias[:, at], ALU.add).then_inc(ps_free, 1)
                    dve.sem_inc(w_free, 1)


def norm_stage(k, src, layer, gain, shift_at, scale_at, tiles, hT, keep_h):
    nc, ins = k.nc, k.ins
    with ExitStack() as ctx:
        sb = sbuf(ctx, nc)
        x = sb("n_x", [P, NT, D])
        sq = sb("n_sq", [P, D])
        g = sb("n_g", [P, D])
        sh = sb("n_sh", [P, 2, D])
        sc = sb("n_sc", [P, 2, D])
        ss = sb("n_ss", [P, NT])
        sd = sb("n_sd", [P, NT])
        rs = sb("n_rs", [P, NT])
        x_in = [k.sem(f"n_x_in{t}") for t in range(tiles)]
        mod_in, squared, var, root, h_ready = (k.sem("n_mod_in"), k.sem("n_squared"), k.sem("n_var"),
                                               k.sem("n_root"), k.sem("n_h_ready"))
        turned, copied, stored = k.sem("n_turned"), k.sem("n_copied"), k.sem("n_stored")
        block = ctx.enter_context(nc.Block())

        @block.sync
        def _(sp):
            for t in range(tiles):
                sp.dma_start(x[:, t, :], src[t]).then_inc(x_in[t], 16)
            sp.dma_start(g[:], gain.partition_broadcast(P)).then_inc(mod_in, 16)
            for r, t in ((0, 0), (1, LAT)):
                for dst, at in ((sh, shift_at), (sc, scale_at)):
                    sp.dma_start(dst[:, r, :], k.mods[layer, t, at * D:(at + 1) * D].partition_broadcast(P)).then_inc(mod_in, 16)
            if keep_h:
                for t in range(tiles):
                    sp.wait_ge(h_ready, t + 1)
                    sp.dma_start(k.h[t], x[:, t, :]).then_inc(stored, 16)
                sp.wait_ge(stored, 16 * tiles)

        @block.scalar
        def _(act):
            for t in range(tiles):
                act.wait_ge(x_in[t], 16)
                if t:
                    act.wait_ge(squared, t)
                nc.scalar.activation(sq[:], x[:, t, :], ACT.Square, accum_out=ss[:, t:t + 1]).then_inc(squared, 1)
            act.wait_ge(var, 1)
            nc.scalar.activation(sd[:, 0:tiles], sd[:, 0:tiles], ACT.Sqrt).then_inc(root, 1)
            for t in range(tiles):
                act.wait_ge(turned, t + 1)
                b = 2 * (t % 2)
                nc.scalar.activation(hT[:, :, t * P:(t + 1) * P],
                                     k.flat[:, b * BANK:(b + 2) * BANK].rearrange("p (k c) -> p k c", k=KD),
                                     ACT.Copy).then_inc(copied, 1)

        @block.vector
        def _(dve):
            dve.wait_ge(mod_in, 16 * 5)
            for r in range(2):
                nc.vector.scalar_tensor_tensor(out=sc[:, r, :], in0=sc[:, r, :], scalar=1.0, in1=g[:],
                                               op0=ALU.add, op1=ALU.mult)
            dve.wait_ge(squared, tiles)
            nc.vector.tensor_scalar(sd[:, 0:tiles], ss[:, 0:tiles], 1.0 / D, EPS, ALU.mult, ALU.add).then_inc(var, 1)
            dve.wait_ge(root, 1)
            nc.vector.reciprocal(rs[:, 0:tiles], sd[:, 0:tiles])
            dve.drain()
            for t in range(tiles):
                r = 0 if t < LAT else 1
                nc.vector.scalar_tensor_tensor(out=x[:, t, :], in0=x[:, t, :], scalar=rs[:, t:t + 1], in1=sc[:, r, :],
                                               op0=ALU.mult, op1=ALU.mult)
                dve.drain()
                nc.vector.tensor_tensor(x[:, t, :], x[:, t, :], sh[:, r, :], ALU.add).then_inc(h_ready, 1)

        @block.tensor
        def _(pe):
            for t in range(tiles):
                pe.wait_ge(h_ready, t + 1)
                if t >= 2:
                    pe.wait_ge(copied, t - 1)
                b = 2 * (t % 2) * BANK
                for kt in range(KD):
                    mm = nc.tensor.transpose(k.flat[:, b + kt * P:b + (kt + 1) * P], x[:, t, kt * P:(kt + 1) * P], k.ident[:])
                mm.then_inc(turned, 1)


def ssd_project_stage(k, hT, w, xb, bct, dt):
    nc, ins = k.nc, k.ins
    PADL = TL + 4
    STRIP = PADL + CTX * P + 4
    OUT = STRIP - 4
    NM, RW = MX + 2 * MB, 4
    TURN = MX + MB
    with ExitStack() as ctx:
        sb = sbuf(ctx, nc)
        wz = sb("ip_wz", [P, 2, KD * BANK])
        wdt = sb("ip_wdt", [P, KD * DH])
        dtb = sb("ip_dtb", [P, DH])
        cw = sb("ip_cw", [P, NM, 5])
        cb = sb("ip_cb", [P, NM])
        pad = sb("ip_pad", [P, 2, STRIP])
        acc = sb("ip_acc", [P, 2, OUT])
        st = sb("ip_st", [P, 2, OUT])
        zs = sb("ip_zs", [P, 2, BANK])
        w_in = [k.sem(f"ip_w_in{s}") for s in range(RW)]
        z_in = [k.sem(f"ip_z_in{s}") for s in range(2)]
        small_in, zeroed = k.sem("ip_small_in"), k.sem("ip_zeroed")
        projected, padded, conved = k.sem("ip_projected"), k.sem("ip_padded"), k.sem("ip_conved")
        activated, turned, kept, turn_read = k.sem("ip_activated"), k.sem("ip_turned"), k.sem("ip_kept"), k.sem("ip_turn_read")
        dt_full, z_full, zs_ready = k.sem("ip_dt_full"), k.sem("ip_z_full"), k.sem("ip_zs_ready")
        z_stored = [k.sem(f"ip_z_stored{q}") for q in range(2)]
        block = ctx.enter_context(nc.Block())

        @block.sync
        def _(sp):
            for m in range(NM):
                if m >= RW:
                    sp.wait_ge(projected, m - RW + 1)
                sp.dma_start(w[:, m % RW, :], ins["w_xbc"][m]).then_inc(w_in[m % RW], 16)
                if m == 1:
                    sp.dma_start(cw[:], ins["conv_w"]).then_inc(small_in, 16)
                    sp.dma_start(cb[:], ins["conv_b"]).then_inc(small_in, 16)
                    sp.dma_start(wdt[:], ins["w_dt"]).then_inc(small_in, 16)
                    sp.dma_start(dtb[:], ins["dt_bias"].partition_broadcast(P)).then_inc(small_in, 16)
            for n in range(4):
                if n >= 2:
                    sp.wait_ge(z_full, (n - 1) * NT)
                sp.dma_start(wz[:, n % 2, :], ins["w_z"][n]).then_inc(z_in[n % 2], 16)
                for t in range(NT):
                    if n >= 1:
                        i = (n - 1) * NT + t
                        sp.wait_ge(zs_ready, i + 1)
                        sp.dma_start(k.z[n - 1, t], zs[:, i % 2, :]).then_inc(z_stored[i % 2], 16)
            for t in range(NT):
                i = 3 * NT + t
                sp.wait_ge(zs_ready, i + 1)
                sp.dma_start(k.z[3, t], zs[:, i % 2, :]).then_inc(z_stored[i % 2], 16)
            for q in range(2):
                sp.wait_ge(z_stored[q], 16 * 2 * NT)

        @block.tensor
        def _(pe):
            def turn(m):
                pe.wait_ge(activated, m + 1)
                if m >= 2:
                    pe.wait_ge(turn_read, m - 1)
                o = (4 + 2 * (m % 2)) * BANK
                for t in range(NT):
                    a = t * P if t < LAT else PADL + (t - LAT) * P
                    mm = nc.tensor.transpose(k.flat[:, o + t * P:o + (t + 1) * P], st[:, m % 2, a:a + P], k.ident[:])
                mm.then_inc(turned, 1)

            for m in range(NM):
                s = m % 2
                pe.wait_ge(w_in[m % RW], 16 * (m // RW + 1))
                if m >= 2:
                    pe.wait_ge(padded, m - 1)
                for kt in range(KD):
                    for o, a, n in ((0, 0, TL), (BANK, TL, CTX * P)):
                        mm = nc.tensor.matmul(k.flat[:, s * 2 * BANK + o:s * 2 * BANK + o + n], w[:, m % RW, kt * P:(kt + 1) * P],
                                              hT[:, kt, a:a + n], start=kt == 0, stop=kt == KD - 1)
                mm.then_inc(projected, 1)
                if 1 <= m <= TURN:
                    turn(m - 1)
            pe.wait_ge(padded, NM)
            pe.wait_ge(small_in, 64)
            for t in range(NT):
                for kt in range(KD):
                    mm = nc.tensor.matmul(k.flat[:, t * DH:(t + 1) * DH], hT[:, kt, t * P:(t + 1) * P], wdt[:, kt * DH:(kt + 1) * DH],
                                          start=kt == 0, stop=kt == KD - 1)
            mm.then_inc(dt_full, 1)
            for n in range(4):
                pe.wait_ge(z_in[n % 2], 16 * (n // 2 + 1))
                for t in range(NT):
                    i = n * NT + t
                    if i >= 2:
                        pe.wait_ge(zs_ready, i - 1)
                    for kt in range(KD):
                        mm = nc.tensor.matmul(k.ps[:, 2 + i % 2, :], hT[:, kt, t * P:(t + 1) * P], wz[:, n % 2, kt * BANK:(kt + 1) * BANK],
                                              start=kt == 0, stop=kt == KD - 1)
                    mm.then_inc(z_full, 1)

        @block.scalar
        def _(act):
            def place(m):
                s = m % 2
                act.wait_ge(projected, m + 1)
                if m >= 2:
                    act.wait_ge(conved, m - 1)
                nc.scalar.activation(pad[:, s, 2:2 + TL], k.flat[:, s * 2 * BANK:s * 2 * BANK + TL], ACT.Copy)
                nc.scalar.activation(pad[:, s, PADL + 2:PADL + 2 + CTX * P],
                                     k.flat[:, (s * 2 + 1) * BANK:(s * 2 + 1) * BANK + CTX * P], ACT.Copy).then_inc(padded, 1)

            def activate(m):
                act.wait_ge(conved, m + 1)
                if m >= 2:
                    if m - 2 < TURN:
                        act.wait_ge(turned, m - 1)
                    if m - 2 >= MX:
                        act.wait_ge(kept, m - 2 - MX + 1)
                nc.scalar.activation(st[:, m % 2, :], acc[:, m % 2, :], ACT.Silu).then_inc(activated, 1)

            def read_turned(m):
                act.wait_ge(turned, m + 1)
                o = (4 + 2 * (m % 2)) * BANK
                nc.scalar.activation(xb[:, :, m * P:(m + 1) * P], k.flat[:, o:o + T].rearrange("p (t c) -> p t c", t=NT),
                                     ACT.Copy).then_inc(turn_read, 1)

            act.wait_ge(zeroed, 1)
            for m in range(NM + 2):
                if m < NM:
                    place(m)
                if 1 <= m <= NM:
                    activate(m - 1)
                if 2 <= m <= TURN + 1:
                    read_turned(m - 2)
            for i in range(4 * NT):
                act.wait_ge(z_full, i + 1)
                if i >= 2:
                    act.wait_ge(z_stored[i % 2], 16 * (i // 2))
                nc.scalar.activation(zs[:, i % 2, :], k.ps[:, 2 + i % 2, :], ACT.Silu).then_inc(zs_ready, 1)

        @block.vector
        def _(dve):
            nc.vector.memset(pad[:], 0.0).then_inc(zeroed, 1)
            dve.wait_ge(small_in, 64)
            for m in range(NM):
                s = m % 2
                dve.wait_ge(padded, m + 1)
                if m >= 2:
                    dve.wait_ge(activated, m - 1)
                nc.vector.tensor_scalar(acc[:, s, :], pad[:, s, 0:OUT], cw[:, m, 0:1], cb[:, m:m + 1], ALU.mult, ALU.add)
                for tap in range(1, 5):
                    dve.drain()
                    last = nc.vector.scalar_tensor_tensor(out=acc[:, s, :], in0=pad[:, s, tap:tap + OUT], scalar=cw[:, m, tap:tap + 1],
                                                          in1=acc[:, s, :], op0=ALU.mult, op1=ALU.add)
                last.then_inc(conved, 1)
            dve.wait_ge(dt_full, 1)
            nc.vector.tensor_tensor(dt[:], k.flat[:, 0:NT * DH].rearrange("p (t c) -> p t c", t=NT),
                                    bcast(dtb[:].unsqueeze(1), [P, NT, DH]), ALU.add)

        @block.gpsimd
        def _(pool):
            for m in range(MX, NM):
                pool.wait_ge(activated, m + 1)
                nc.gpsimd.tensor_copy(bct[:, m - MX, 0:TL], st[:, m % 2, 0:TL])
                nc.gpsimd.tensor_copy(bct[:, m - MX, TL:T], st[:, m % 2, PADL:PADL + CTX * P]).then_inc(kept, 1)


def ssd_scan_stage(k, xb, bct, dt, y):
    nc, ins = k.nc, k.ins
    AHEAD = 2
    WS = 2 * (AHEAD + 1)
    with ExitStack() as ctx:
        sb = sbuf(ctx, nc)
        a = sb("sc_a", [P, DH])
        dsk = sb("sc_d", [P, DH])
        tmp = [sb(f"sc_tmp{i}", [P, NT * DH]) for i in range(3)]
        dta = sb("sc_dta", [P, NT, DH])
        cs = sb("sc_cs", [P, NT, DH])
        ncs = sb("sc_ncs", [P, NT, DH])
        ecs = sb("sc_ecs", [P, NT, DH])
        etot = sb("sc_etot", [P, NT, DH])
        wend = sb("sc_wend", [P, NT, DH])
        dsum = sb("sc_dsum", [P, HEADS])
        state = sb("sc_state", [P, DI])
        xdt = sb("sc_xdt", [P, 2, DI])
        xw = sb("sc_xw", [P, DI])
        cbm = sb("sc_cbm", [P, AHEAD + 1, P])
        seg = sb("sc_seg", [P, 4, BANK])
        w = sb("sc_w", [P, WS, BANK])
        off = sb("sc_off", [P, BANK])
        small_in = k.sem("sc_small_in")
        pre = {n: k.sem(f"sc_{n}") for n in ("decay", "absolute", "exped", "dta", "sums", "cs", "ecs", "ready", "y0")}
        xdt_ready, xw_ready, zero_state = k.sem("sc_xdt_ready"), k.sem("sc_xw_ready"), k.sem("sc_zero_state")
        cb_full, cb_masked = k.sem("sc_cb_full"), k.sem("sc_cb_masked")
        row_full, clamped, exped, weighed = k.sem("sc_row_full"), k.sem("sc_clamped"), k.sem("sc_exped"), k.sem("sc_weighed")
        y_full, y_read, s_full, s_read = k.sem("sc_y_full"), k.sem("sc_y_read"), k.sem("sc_s_full"), k.sem("sc_s_read")
        block = ctx.enter_context(nc.Block())
        steps = [(0, c) for c in (4, 5, 0, 1, 2, 3)] + [(1, c) for c in (5, 4, 3, 2, 1, 0)]
        NS = len(steps)
        flat = lambda t: t[:].rearrange("p t c -> p (t c)")

        @block.sync
        def _(sp):
            sp.dma_start(a[:], ins["a_log"].partition_broadcast(P)).then_inc(small_in, 16)
            sp.dma_start(dsk[:], ins["ssd_d"].partition_broadcast(P)).then_inc(small_in, 16)

        @block.scalar
        def _(act):
            act.wait_ge(small_in, 32)
            nc.scalar.activation(a[:], a[:], ACT.Exp).then_inc(pre["decay"], 1)
            act.wait_ge(pre["absolute"], 1)
            nc.scalar.activation(tmp[1][:], tmp[0][:], ACT.Exp, scale=-1.0).then_inc(pre["exped"], 1)
            act.wait_ge(pre["cs"], 1)
            nc.scalar.activation(flat(ecs), flat(cs), ACT.Exp)
            nc.scalar.activation(flat(wend), flat(wend), ACT.Exp)
            nc.scalar.activation(flat(etot), flat(etot), ACT.Exp).then_inc(pre["ecs"], 1)
            for i, (d, c) in enumerate(steps):
                for q in range(2 * GROUPS):
                    n = i * 2 * GROUPS + q
                    act.wait_ge(clamped, n + 1)
                    if n >= WS:
                        act.wait_ge(y_full, (n - WS) // 2 + 1)
                    for r in range(4):
                        h = d * HEADS + q * 4 + r
                        last = nc.scalar.activation(w[:, n % WS, r * P:(r + 1) * P], seg[:, n % 4, r * P:(r + 1) * P], ACT.Exp,
                                                    bias=ncs[:, c, h:h + 1])
                    last.then_inc(exped, 1)

        @block.gpsimd
        def _(pool):
            pool.wait_ge(pre["ready"], 1)
            for c in range(NT):
                last = nc.gpsimd.tensor_tensor(y[:, c, :].rearrange("p (h e) -> p h e", h=HEADS),
                                               xb[:, c, 0:DI].rearrange("p (h e) -> p h e", h=HEADS),
                                               bcast(dsum[:].unsqueeze(2), [P, HEADS, HD]), ALU.mult)
                last.then_inc(pre["y0"], 1)

            def scale_x(i):
                d, c = steps[i]
                if i >= 2:
                    pool.wait_ge(y_full, (i - 1) * GROUPS)
                nc.gpsimd.tensor_tensor(xdt[:, i % 2, :].rearrange("p (h e) -> p h e", h=HEADS),
                                        xb[:, c, 0:DI].rearrange("p (h e) -> p h e", h=HEADS),
                                        bcast(dt[:, c, d * HEADS:(d + 1) * HEADS].unsqueeze(2), [P, HEADS, HD]),
                                        ALU.mult).then_inc(xdt_ready, 1)

            scale_x(0)
            for i, (d, c) in enumerate(steps):
                if i + 1 < NS:
                    scale_x(i + 1)
                for q in range(2 * GROUPS):
                    n = i * 2 * GROUPS + q
                    g = i * GROUPS + q // 2
                    pool.wait_ge(exped, n + 1)
                    pool.wait_ge(cb_masked, g + 1)
                    nc.gpsimd.tensor_tensor(w[:, n % WS, :].rearrange("p (r e) -> p r e", r=4),
                                            w[:, n % WS, :].rearrange("p (r e) -> p r e", r=4),
                                            bcast(cbm[:, g % (AHEAD + 1), :].unsqueeze(1), [P, 4, P]), ALU.mult).then_inc(weighed, 1)

        @block.tensor
        def _(pe):
            pe.wait_ge(pre["dta"], 1)
            for o, m in ((0, k.tri[:, 0, :]), (1, k.tri[:, 1, :]), (2, k.ones[:])):
                mm = nc.tensor.matmul(k.ps[:, o, 0:NT * DH], m, flat(dta), start=True, stop=True)
            mm.then_inc(pre["sums"], 1)
            pe.wait_ge(pre["ready"], 1)
            def front(G):
                (d, c), g = steps[G // GROUPS], G % GROUPS
                if G >= 1:
                    pe.wait_ge(cb_masked, G)
                nc.tensor.matmul(k.ps[:, 2, 0:P], bct[:, g, c * P:(c + 1) * P], bct[:, MB + g, c * P:(c + 1) * P],
                                 start=True, stop=True).then_inc(cb_full, 1)
                for n in (2 * G, 2 * G + 1):
                    if n >= 2:
                        pe.wait_ge(clamped, n - 1)
                    for r in range(4):
                        h = d * HEADS + g * HPG + (n % 2) * 4 + r
                        mm = nc.tensor.matmul(k.ps[:, n % 2, r * P:(r + 1) * P], bcast(dta[:, c, h:h + 1], [P, P]), k.tri[:, d, :],
                                              start=True, stop=True)
                    mm.then_inc(row_full, 1)

            def back(G):
                i, g = G // GROUPS, G % GROUPS
                d, c = steps[i]
                if G >= 1:
                    pe.wait_ge(y_read, G)
                if i in (0, NT):
                    pe.wait_ge(zero_state, 1 + i // NT)
                else:
                    pe.wait_ge(s_read, G - GROUPS + 1)
                nc.tensor.matmul(k.ps[:, 5, :], bct[:, MB + g, c * P:(c + 1) * P], state[:, g * BANK:(g + 1) * BANK], start=True, stop=True)
                pe.wait_ge(xw_ready, i + 1)
                if G >= 2:
                    pe.wait_ge(s_read, G - 1)
                nc.tensor.matmul(k.ps[:, 6 + G % 2, :], xb[:, c, DI + g * P:DI + (g + 1) * P], xw[:, g * BANK:(g + 1) * BANK],
                                 start=True, stop=True).then_inc(s_full, 1)
                pe.wait_ge(xdt_ready, i + 1)
                for n in (2 * G, 2 * G + 1):
                    pe.wait_ge(weighed, n + 1)
                    for r in range(4):
                        e = ((n % 2) * 4 + r) * HD
                        mm = nc.tensor.matmul(k.ps[:, 3 + G % 2, e:e + HD], w[:, n % WS, r * P:(r + 1) * P],
                                              xdt[:, i % 2, g * BANK + e:g * BANK + e + HD], start=True, stop=True)
                mm.then_inc(y_full, 1)

            for G in range(NS * GROUPS + AHEAD):
                if G < NS * GROUPS:
                    front(G)
                if G >= AHEAD:
                    back(G - AHEAD)

        @block.vector
        def _(dve):
            dve.wait_ge(small_in, 32)
            v = flat(dt)
            nc.vector.scalar_tensor_tensor(out=tmp[0][:], in0=v, scalar=-1.0, in1=v, op0=ALU.mult, op1=ALU.max).then_inc(pre["absolute"], 1)
            dve.wait_ge(pre["exped"], 1)
            nc.vector.tensor_scalar(tmp[2][:], tmp[1][:], 2.0, None, ALU.add)
            dve.drain()
            nc.vector.reciprocal(tmp[2][:], tmp[2][:])
            dve.drain()
            nc.vector.tensor_tensor(tmp[1][:], tmp[1][:], tmp[2][:], ALU.mult)
            dve.drain()
            nc.vector.tensor_tensor(tmp[2][:], tmp[1][:], tmp[1][:], ALU.mult)
            dve.drain()
            nc.vector.tensor_scalar(tmp[0][:], tmp[2][:], 1.0 / 17, None, ALU.mult)
            for odd in (15, 13, 11, 9, 7, 5, 3):
                dve.drain()
                nc.vector.scalar_tensor_tensor(out=tmp[0][:], in0=tmp[0][:], scalar=1.0 / odd, in1=tmp[2][:], op0=ALU.add, op1=ALU.mult)
            dve.drain()
            nc.vector.scalar_tensor_tensor(out=tmp[0][:], in0=tmp[0][:], scalar=1.0, in1=tmp[1][:], op0=ALU.add, op1=ALU.mult)
            nc.vector.tensor_scalar(tmp[2][:], v, 0.0, None, ALU.max)
            dve.drain()
            nc.vector.scalar_tensor_tensor(out=v, in0=tmp[0][:], scalar=2.0, in1=tmp[2][:], op0=ALU.mult, op1=ALU.add)
            nc.vector.tensor_tensor(dsum[:], dsk[:, 0:HEADS], dsk[:, HEADS:DH], ALU.add)
            dve.wait_ge(pre["decay"], 1)
            dve.drain()
            nc.vector.scalar_tensor_tensor(out=dta[:], in0=dt[:], scalar=-1.0, in1=bcast(a[:].unsqueeze(1), [P, NT, DH]),
                                           op0=ALU.mult, op1=ALU.mult).then_inc(pre["dta"], 1)
            dve.wait_ge(pre["sums"], 1)
            sums = [k.ps[:, o, 0:NT * DH].rearrange("p (t c) -> p t c", t=NT) for o in range(3)]
            nc.vector.tensor_copy(cs[:, :, 0:HEADS], sums[0][:, :, 0:HEADS])
            nc.vector.tensor_copy(cs[:, :, HEADS:DH], sums[1][:, :, HEADS:DH])
            nc.vector.tensor_copy(etot[:], sums[2])
            dve.drain()
            nc.vector.tensor_tensor(wend[:], etot[:], cs[:], ALU.subtract)
            nc.vector.tensor_scalar(ncs[:], cs[:], -1.0, None, ALU.mult).then_inc(pre["cs"], 1)
            dve.wait_ge(pre["cs"], 1)
            dve.wait_ge(pre["ecs"], 1)
            nc.vector.tensor_tensor(wend[:], wend[:], dt[:], ALU.mult)
            nc.vector.memset(state[:], 0.0).then_inc(zero_state, 1)
            dve.drain()
            dve.sem_inc(pre["ready"], 1)
            heads = lambda t: t.rearrange("p (h e) -> p h e", h=HPG)

            def front(G):
                i, g = G // GROUPS, G % GROUPS
                d, c = steps[i]
                dve.wait_ge(cb_full, G + 1)
                if G > AHEAD:
                    dve.wait_ge(weighed, 2 * (G - AHEAD))
                nc.vector.tensor_tensor(cbm[:, G % (AHEAD + 1), :], k.ps[:, 2, 0:P], k.tri[:, d, :], ALU.mult).then_inc(cb_masked, 1)
                for n in (2 * G, 2 * G + 1):
                    dve.wait_ge(row_full, n + 1)
                    if n >= 4:
                        dve.wait_ge(exped, n - 3)
                    h = d * HEADS + g * HPG + (n % 2) * 4
                    nc.vector.tensor_tensor(seg[:, n % 4, :].rearrange("p (r e) -> p r e", r=4),
                                            k.ps[:, n % 2, :].rearrange("p (r e) -> p r e", r=4),
                                            bcast(cs[:, c, h:h + 4].unsqueeze(2), [P, 4, P]), ALU.min).then_inc(clamped, 1)

            def back(G):
                i, g = G // GROUPS, G % GROUPS
                d, c = steps[i]
                if g == 0:
                    if i:
                        dve.wait_ge(s_full, G)
                    nc.vector.tensor_tensor(xw[:].rearrange("p (h e) -> p h e", h=HEADS), xb[:, c, 0:DI].rearrange("p (h e) -> p h e", h=HEADS),
                                            bcast(wend[:, c, d * HEADS:(d + 1) * HEADS].unsqueeze(2), [P, HEADS, HD]), ALU.mult).then_inc(xw_ready, 1)
                    if i == NT:
                        dve.wait_ge(s_read, G)
                        nc.vector.memset(state[:], 0.0).then_inc(zero_state, 1)
                hs = slice(d * HEADS + g * HPG, d * HEADS + (g + 1) * HPG)
                cols = slice(g * BANK, (g + 1) * BANK)
                dve.wait_ge(s_full, G + 1)
                dve.wait_ge(y_full, G + 1)
                if G == 0:
                    dve.wait_ge(pre["y0"], NT)
                nc.vector.tensor_tensor(heads(off[:]), heads(k.ps[:, 5, :]),
                                        bcast(ecs[:, c, hs].unsqueeze(2), [P, HPG, HD]), ALU.mult)
                nc.vector.tensor_tensor(y[:, c, cols], y[:, c, cols], k.ps[:, 3 + G % 2, :], ALU.add)
                nc.vector.tensor_tensor(heads(state[:, cols]), heads(state[:, cols]),
                                        bcast(etot[:, c, hs].unsqueeze(2), [P, HPG, HD]), ALU.mult)
                dve.drain()
                nc.vector.tensor_tensor(y[:, c, cols], y[:, c, cols], off[:], ALU.add).then_inc(y_read, 1)
                nc.vector.tensor_tensor(state[:, cols], state[:, cols], k.ps[:, 6 + G % 2, :], ALU.add).then_inc(s_read, 1)

            for G in range(NS * GROUPS + AHEAD):
                if G < NS * GROUPS:
                    front(G)
                if G >= AHEAD:
                    back(G - AHEAD)


def ssd_output_stage(k, y, src, dst):
    nc, ins = k.nc, k.ins
    with ExitStack() as ctx:
        sb = sbuf(ctx, nc)
        w = sb("so_w", [P, MX, D])
        ng = sb("so_ng", [P, MX])
        zt = sb("so_z", [P, 2, DI])
        junk = sb("so_junk", [P, DI])
        sq = sb("so_sq", [P, D])
        yT = sb("so_yT", [P, 2, MX, P])
        x = sb("so_x", [P, 2, D])
        gate = sb("so_gate", [P, 2, D])
        ss, sd, rs = sb("so_ss", [P, NT]), sb("so_sd", [P, NT]), sb("so_rs", [P, NT])
        w_in, small_in = k.sem("so_w_in"), k.sem("so_small_in")
        z_in = [k.sem(f"so_z_in{s}") for s in range(2)]
        x_in = [k.sem(f"so_x_in{s}") for s in range(2)]
        gated, squared, mean, root, inv = (k.sem("so_gated"), k.sem("so_squared"), k.sem("so_mean"), k.sem("so_root"), k.sem("so_inv"))
        turned, copied, full, added = k.sem("so_turned"), k.sem("so_copied"), k.sem("so_full"), k.sem("so_added")
        stored = [k.sem(f"so_stored{s}") for s in range(2)]
        block = ctx.enter_context(nc.Block())

        @block.sync
        def _(sp):
            def load_z(t):
                if t >= 2:
                    sp.wait_ge(gated, t - 1)
                sp.dma_start(zt[:, t % 2, :].rearrange("p (n c) -> p n c", n=4), k.z[:, t].rearrange("n p c -> p n c")).then_inc(z_in[t % 2], 16)

            def load_x(t):
                if t >= 2:
                    sp.wait_ge(stored[t % 2], 16 * (t // 2))
                sp.dma_start(x[:, t % 2, :], src[t]).then_inc(x_in[t % 2], 16)

            load_z(0)
            load_z(1)
            load_x(0)
            load_x(1)
            sp.dma_start(w[:], ins["ssd_out_w"]).then_inc(w_in, 16)
            sp.dma_start(ng[:], ins["ssd_norm_g"]).then_inc(small_in, 16)
            for r, t in ((0, 0), (1, LAT)):
                sp.dma_start(gate[:, r, :], k.mods[0, t, 2 * D:3 * D].partition_broadcast(P)).then_inc(small_in, 16)
            for t in range(NT):
                if t + 2 < NT:
                    load_z(t + 2)
                sp.wait_ge(added, t + 1)
                sp.dma_start(dst[t], x[:, t % 2, :]).then_inc(stored[t % 2], 16)
                if t + 2 < NT:
                    load_x(t + 2)
            for s in range(2):
                sp.wait_ge(stored[s], 16 * NT // 2)

        @block.vector
        def _(dve):
            def gate_tile(t):
                dve.wait_ge(z_in[t % 2], 16 * (t // 2 + 1))
                nc.vector.tensor_tensor(y[:, t, :], y[:, t, :], zt[:, t % 2, :], ALU.mult).then_inc(gated, 1)

            def scale_turned(t):
                if t >= 2:
                    dve.wait_ge(full, t - 1)
                for q in range(4):
                    n = t * 4 + q
                    dve.wait_ge(turned, n + 1)
                    nc.vector.tensor_tensor(yT[:, t % 2, 4 * q:4 * q + 4, :], k.ps[:, n % 4, :].rearrange("p (m c) -> p m c", m=4),
                                            bcast(ng[:, 4 * q:4 * q + 4].unsqueeze(2), [P, 4, P]), ALU.mult).then_inc(copied, 1)

            gate_tile(0)
            dve.wait_ge(small_in, 48)
            gate_tile(1)
            scale_turned(0)
            for t in range(NT):
                if t + 2 < NT:
                    gate_tile(t + 2)
                if t + 1 < NT:
                    scale_turned(t + 1)
                dve.wait_ge(squared, t + 1)
                nc.vector.tensor_scalar(sd[:, t:t + 1], ss[:, t:t + 1], 1.0 / DI, EPS, ALU.mult, ALU.add).then_inc(mean, 1)
                dve.wait_ge(root, t + 1)
                nc.vector.reciprocal(rs[:, t:t + 1], sd[:, t:t + 1])
                r = 0 if t < LAT else 1
                dve.wait_ge(full, t + 1)
                dve.drain()
                b = 4 + 2 * (t % 2)
                nc.vector.scalar_tensor_tensor(out=sq[:], in0=k.flat[:, b * BANK:(b + 2) * BANK], scalar=rs[:, t:t + 1], in1=gate[:, r, :],
                                               op0=ALU.mult, op1=ALU.mult)
                dve.wait_ge(x_in[t % 2], 16 * (t // 2 + 1))
                dve.drain()
                nc.vector.tensor_tensor(x[:, t % 2, :], x[:, t % 2, :], sq[:], ALU.add).then_inc(added, 1)

        @block.scalar
        def _(act):
            for t in range(NT):
                act.wait_ge(gated, t + 1)
                nc.scalar.activation(junk[:], y[:, t, :], ACT.Square, accum_out=ss[:, t:t + 1]).then_inc(squared, 1)
                act.wait_ge(mean, t + 1)
                nc.scalar.activation(sd[:, t:t + 1], sd[:, t:t + 1], ACT.Sqrt).then_inc(root, 1)

        @block.tensor
        def _(pe):
            def turn(t):
                pe.wait_ge(gated, t + 1)
                for q in range(4):
                    n = t * 4 + q
                    if n >= 4:
                        pe.wait_ge(copied, n - 3)
                    for m in range(4):
                        mm = nc.tensor.transpose(k.ps[:, n % 4, m * P:(m + 1) * P], y[:, t, (4 * q + m) * P:(4 * q + m + 1) * P], k.ident[:])
                    mm.then_inc(turned, 1)

            turn(0)
            for t in range(NT):
                if t + 1 < NT:
                    turn(t + 1)
                if t >= 2:
                    pe.wait_ge(added, t - 1)
                if t == 0:
                    pe.wait_ge(w_in, 16)
                pe.wait_ge(copied, (t + 1) * 4)
                b = 4 + 2 * (t % 2)
                for n in range(2):
                    for m in range(MX):
                        mm = nc.tensor.matmul(k.ps[:, b + n, :], yT[:, t % 2, m, :], w[:, m, n * BANK:(n + 1) * BANK], start=m == 0, stop=m == MX - 1)
                mm.then_inc(full, 1)


def select_stage(k, layer, tiles, hT, ids, gates):
    nc, ins = k.nc, k.ins
    RW = 4
    N = tiles * P
    with ExitStack() as ctx:
        sb = sbuf(ctx, nc)
        w = sb("se_w", [P, RW, KD * P])
        keys = sb("se_keys", [P, HC, NKEYS])
        qT = sb("se_qT", [P, 2, NT * P])
        rest = sb("se_rest", [P, NT, NKEYS])
        top = sb("se_top", [P, NT, 2, TOPK])
        topi = sb("se_topi", [P, NT, 2, TOPK], U32)
        topf = sb("se_topf", [P, NT, 2, TOPK])
        cand = sb("se_cand", [P, NT, TOPK * TOPK])
        crest = sb("se_crest", [P, NT, TOPK * TOPK])
        pos = sb("se_pos", [P, NT, TOPK], U32)
        part = sb("se_part", [P, 2, NT, TOPK], U32)
        partf = sb("se_partf", [P, 2, NT, TOPK])
        hot = sb("se_hot", [P, NT, TOPK, TOPK])
        half = sb("se_half", [P, 2, NT, TOPK])
        best = sb("se_best", [P, NT, PH, TOPK])
        idf = sb("se_idf", [P, NT, PH, TOPK])
        tot = sb("se_tot", [P, NT * PH])
        iota = sb("se_iota", [P, TOPK])
        w_in = [k.sem(f"se_w_in{s}") for s in range(RW)]
        small_in = k.sem("se_small_in")
        projected, q_ready, scored, ranked = k.sem("se_projected"), k.sem("se_q_ready"), k.sem("se_scored"), k.sem("se_ranked")
        shifted, exped = k.sem("se_shifted"), k.sem("se_exped")
        block = ctx.enter_context(nc.Block())

        @block.sync
        def _(sp):
            for m in range(HC):
                if m >= RW:
                    sp.wait_ge(projected, m - RW + 1)
                sp.dma_start(w[:, m % RW, :], ins["peer_q_w"][layer, m]).then_inc(w_in[m % RW], 16)
                if m == 0:
                    sp.dma_start(keys[:], ins["peer_keys"][layer]).then_inc(small_in, 16)
                    sp.dma_start(iota[:], ins["iota"].partition_broadcast(P)).then_inc(small_in, 16)

        @block.tensor
        def _(pe):
            def score(m):
                pe.wait_ge(q_ready, m + 1)
                if m >= 2:
                    pe.wait_ge(ranked, m - 1)
                for t in range(tiles):
                    o = (4 + 2 * (m % 2)) * BANK + t * P
                    mm = nc.tensor.matmul(k.flat[:, o:o + P], qT[:, m % 2, t * P:(t + 1) * P], keys[:, m, :], start=True, stop=True)
                mm.then_inc(scored, 1)

            pe.wait_ge(small_in, 32)
            for m in range(HC + 1):
                if m < HC:
                    pe.wait_ge(w_in[m % RW], 16 * (m // RW + 1))
                    if m >= 2:
                        pe.wait_ge(q_ready, m - 1)
                    for kt in range(KD):
                        for o in range(0, N, BANK):
                            n = min(BANK, N - o)
                            mm = nc.tensor.matmul(k.flat[:, (m % 2) * 2 * BANK + o:(m % 2) * 2 * BANK + o + n], w[:, m % RW, kt * P:(kt + 1) * P],
                                                  hT[:, kt, o:o + n], start=kt == 0, stop=kt == KD - 1)
                    mm.then_inc(projected, 1)
                if m:
                    score(m - 1)

        @block.scalar
        def _(act):
            for m in range(HC):
                act.wait_ge(projected, m + 1)
                if m >= 2:
                    act.wait_ge(scored, m - 1)
                nc.scalar.activation(qT[:, m % 2, 0:N], k.flat[:, (m % 2) * 2 * BANK:(m % 2) * 2 * BANK + N], ACT.Copy).then_inc(q_ready, 1)
            act.wait_ge(shifted, 1)
            nc.scalar.activation(best[:, 0:tiles], best[:, 0:tiles], ACT.Exp).then_inc(exped, 1)

        @block.vector
        def _(dve):
            V = nc.vector
            tt = range(tiles)

            def top16(vals, rest, out_v, out_i):
                for t in tt:
                    V.max(out_v(t, 0), vals(t))
                dve.drain()
                for t in tt:
                    V.max_index(out_i(t, 0), out_v(t, 0), vals(t))
                    V.match_replace(rest(t), out_v(t, 0), vals(t), NEG)
                dve.drain()
                for t in tt:
                    V.max(out_v(t, 1), rest(t))
                dve.drain()
                for t in tt:
                    last = V.max_index(out_i(t, 1), out_v(t, 1), rest(t))
                return last

            dve.wait_ge(small_in, 32)
            for m in range(HC):
                c, h = m % 2, m // 2
                dve.wait_ge(scored, m + 1)
                o = (4 + 2 * (m % 2)) * BANK
                top16(lambda t: k.flat[:, o + t * P:o + (t + 1) * P], lambda t: rest[:, t, :],
                      lambda t, j: top[:, t, c, 8 * j:8 * j + 8], lambda t, j: topi[:, t, c, 8 * j:8 * j + 8]).then_inc(ranked, 1)
                if c == 0:
                    continue
                dve.drain()
                V.tensor_copy(topf[:, 0:tiles], topi[:, 0:tiles])
                V.tensor_tensor(cand[:, 0:tiles].rearrange("p t (a b) -> p t a b", a=TOPK),
                                bcast(top[:, 0:tiles, 0, :].unsqueeze(3), [P, tiles, TOPK, TOPK]),
                                bcast(top[:, 0:tiles, 1, :].unsqueeze(2), [P, tiles, TOPK, TOPK]), ALU.add)
                dve.drain()
                top16(lambda t: cand[:, t, :], lambda t: crest[:, t, :],
                      lambda t, j: best[:, t, h, 8 * j:8 * j + 8], lambda t, j: pos[:, t, 8 * j:8 * j + 8])
                dve.drain()
                V.tensor_scalar(part[:, 0, 0:tiles], pos[:, 0:tiles], 4, None, ALU.logical_shift_right)
                V.tensor_scalar(part[:, 1, 0:tiles], pos[:, 0:tiles], 15, None, ALU.bitwise_and)
                dve.drain()
                V.tensor_copy(partf[:, :, 0:tiles], part[:, :, 0:tiles])
                for c in range(2):
                    dve.drain()
                    V.tensor_tensor(hot[:, 0:tiles], bcast(partf[:, c, 0:tiles].unsqueeze(3), [P, tiles, TOPK, TOPK]),
                                    bcast(iota[:].unsqueeze(1).unsqueeze(1), [P, tiles, TOPK, TOPK]), ALU.is_equal)
                    dve.drain()
                    V.tensor_tensor(hot[:, 0:tiles], hot[:, 0:tiles], bcast(topf[:, 0:tiles, c, :].unsqueeze(2), [P, tiles, TOPK, TOPK]), ALU.mult)
                    dve.drain()
                    V.tensor_reduce(half[:, c, 0:tiles], hot[:, 0:tiles], AX.X, ALU.add)
                dve.drain()
                V.scalar_tensor_tensor(out=idf[:, 0:tiles, h, :], in0=half[:, 0, 0:tiles], scalar=float(NKEYS), in1=half[:, 1, 0:tiles],
                                       op0=ALU.mult, op1=ALU.add)
            dve.drain()
            V.tensor_copy(ids[:, 0:tiles], idf[:, 0:tiles])
            rows = best[:, 0:tiles].rearrange("p t h e -> p (t h) e")
            V.tensor_copy(tot[:, 0:tiles * PH], best[:, 0:tiles, :, 0].rearrange("p t h -> p (t h)"))
            dve.drain()
            V.tensor_tensor(rows, rows, bcast(tot[:, 0:tiles * PH].unsqueeze(2), [P, tiles * PH, TOPK]), ALU.subtract).then_inc(shifted, 1)
            dve.wait_ge(exped, 1)
            V.tensor_reduce(tot[:, 0:tiles * PH], rows, AX.X, ALU.add)
            dve.drain()
            V.reciprocal(tot[:, 0:tiles * PH], tot[:, 0:tiles * PH])
            dve.drain()
            V.tensor_tensor(gates[:, 0:tiles].rearrange("p t h e -> p (t h) e"), rows,
                            bcast(tot[:, 0:tiles * PH].unsqueeze(2), [P, tiles * PH, TOPK]), ALU.mult)


def expert_stage(k, layer, tiles, ids, gates, src, dst):
    nc, ins = k.nc, k.ins
    E = TOPK
    with ExitStack() as ctx:
        sb = sbuf(ctx, nc)
        ring = sb("ex_ring", [P, SLOTS, 2 * D])
        idx = sb("ex_idx", [P, E], U32)
        gate = sb("ex_gate", [P, E])
        dot, act_out, weight = sb("ex_dot", [P, E]), sb("ex_act", [P, E]), sb("ex_weight", [P, E])
        hn, h = sb("ex_h_next", [P, D]), sb("ex_h", [P, D])
        acc, x, g2, out = sb("ex_acc", [P, D]), sb("ex_x", [P, D]), sb("ex_g2", [P, D]), sb("ex_out", [P, D])
        landed = [k.sem(f"ex_landed{s}") for s in range(SLOTS)]
        slot_free, staged, may_gather = k.sem("ex_slot_free"), k.sem("ex_staged"), k.sem("ex_may_gather")
        h_in, h_free, x_in, x_free = k.sem("ex_h_in"), k.sem("ex_h_free"), k.sem("ex_x_in"), k.sem("ex_x_free")
        dotted, gelued, weighted = k.sem("ex_dotted"), k.sem("ex_gelued"), k.sem("ex_weighted")
        out_ready, out_free, stored = k.sem("ex_out_ready"), k.sem("ex_out_free"), k.sem("ex_stored")
        block = ctx.enter_context(nc.Block())
        flat = lambda a: a[:].rearrange("p t h e -> p (t h e)")

        @block.gpsimd
        def _(pool):
            with pool.Fori(0, tiles * PH) as i:
                for e in range(E):
                    k.hold(pool, "pool", slot_free, i * E + e + 1)
                    if e % 8 == 0:
                        nc.gpsimd.tensor_copy(gate[:, e:e + 8], flat(gates)[:, bass.ds(i * E + e, 8)])
                        nc.gpsimd.tensor_copy(idx[:, e:e + 8], flat(ids)[:, bass.ds(i * E + e, 8)]).then_inc(staged, 1)
                        k.hold(pool, "pool", staged, i * 2 + e // 8 + 1)
                    pool.indirect_dma_start(out=ring[:, e % SLOTS, :], out_offset=None, in_=ins[f"peer_uv{layer}"],
                                            in_offset=bass.IndirectOffsetOnAxis(ap=idx[:, e:e + 1], axis=0)).then_inc(landed[e % SLOTS], 16)

        @block.sync
        def _(sp):
            sp.sem_inc(out_free, 1)
            with sp.Fori(0, tiles) as b:
                sp.wait_ge(h_free, b + 1)
                sp.dma_start(hn[:], k.h[bass.ds(b, 1)].rearrange("o p n -> (o p) n")).then_inc(h_in, 16)
                sp.wait_ge(x_free, b + 1)
                sp.dma_start(x[:], src[bass.ds(b, 1)].rearrange("o p n -> (o p) n")).then_inc(x_in, 16)
                sp.dma_start(g2[:], k.mods[layer, bass.ds(b, 1), 5 * D:6 * D].rearrange("o n -> (o n)").partition_broadcast(P)).then_inc(x_in, 16)
                sp.wait_ge(out_ready, b + 1)
                sp.dma_start(dst[bass.ds(b, 1)].rearrange("o p n -> (o p) n"), out[:]).then_inc(stored, 16)
                k.hold(sp, "sp", stored, (b + 1) * 16)
                sp.sem_inc(out_free, 1)
            sp.wait_ge(stored, 16 * tiles)

        @block.scalar
        def _(act):
            with act.Fori(0, tiles * PH) as i:
                for e in range(E):
                    n = i * E + e + 1
                    act.wait_ge(dotted, n)
                    nc.scalar.activation(act_out[:, e:e + 1], dot[:, e:e + 1], ACT.Gelu).then_inc(gelued, 1)
                    act.wait_ge(gelued, n)
                    nc.scalar.activation(weight[:, e:e + 1], act_out[:, e:e + 1], ACT.Copy, scale=gate[:, e:e + 1]).then_inc(weighted, 1)

        @block.vector
        def _(dve):
            dve.sem_inc(slot_free, SLOTS)
            dve.sem_inc(h_free, 1)
            dve.sem_inc(x_free, 1)

            def add_expert(i, e):
                dve.wait_ge(slot_free, i * E + e + SLOTS)
                dve.wait_ge(weighted, i * E + e + 1)
                nc.vector.scalar_tensor_tensor(out=acc[:], in0=ring[:, e % SLOTS, D:2 * D], scalar=weight[:, e:e + 1], in1=acc[:],
                                               op0=ALU.mult, op1=ALU.add).then_inc(slot_free, 1)

            with dve.Fori(0, tiles) as b:
                k.hold(dve, "dve", h_in, (b + 1) * 16)
                nc.vector.tensor_copy(h[:], hn[:])
                nc.vector.memset(acc[:], 0.0)
                dve.drain()
                dve.sem_inc(h_free, 1)
                with dve.Fori(0, PH) as head:
                    i = b * PH + head
                    for e in range(E):
                        dve.wait_ge(landed[e % SLOTS], i * 32 + 16 * (e // SLOTS + 1))
                        nc.vector.tensor_tensor_reduce(out=ring[:, e % SLOTS, 0:D], in0=ring[:, e % SLOTS, 0:D], in1=h[:], scale=1.0, scalar=0.0,
                                                       op0=ALU.mult, op1=ALU.add, accum_out=dot[:, e:e + 1]).then_inc(dotted, 1)
                        if e:
                            add_expert(i, e - 1)
                    add_expert(i, E - 1)
                dve.drain()
                k.hold(dve, "dve", x_in, (b + 1) * 32)
                k.hold(dve, "dve", out_free, b + 1)
                nc.vector.tensor_tensor(out[:], acc[:], g2[:], ALU.mult)
                dve.drain()
                nc.vector.tensor_tensor(out[:], out[:], x[:], ALU.add).then_inc(out_ready, 1)
                dve.drain()
                dve.sem_inc(x_free, 1)


def attention_project_stage(k, hT, qT, kT, v):
    nc, ins = k.nc, k.ins
    RW = 4
    with ExitStack() as ctx:
        sb = sbuf(ctx, nc)
        w = sb("ap_w", [P, RW, KD * P])
        wv = sb("ap_wv", [P, 2, KD * BANK])
        rope = sb("ap_rope", [P, 2, TL])
        rot = sb("ap_rot", [P, P])
        raw = sb("ap_raw", [P, 2, TL])
        rs = sb("ap_rs", [P, 2, TL])
        w_in = [k.sem(f"ap_w_in{s}") for s in range(RW)]
        wv_in, small_in = k.sem("ap_wv_in"), k.sem("ap_small_in")
        projected, raw_ready, rotated, done = k.sem("ap_projected"), k.sem("ap_raw_ready"), k.sem("ap_rotated"), k.sem("ap_done")
        v_full, v_read = k.sem("ap_v_full"), k.sem("ap_v_read")
        block = ctx.enter_context(nc.Block())
        NM = 2 * AH

        @block.sync
        def _(sp):
            for m in range(NM):
                if m >= RW:
                    sp.wait_ge(projected, m - RW + 1)
                sp.dma_start(w[:, m % RW, :], ins["w_qk"][m]).then_inc(w_in[m % RW], 16)
                if m == 0:
                    sp.dma_start(rope[:], ins["rope"]).then_inc(small_in, 16)
                    sp.dma_start(rot[:], ins["rot"]).then_inc(small_in, 16)
            for n in range(2):
                sp.dma_start(wv[:, n, :], ins["w_v"][n]).then_inc(wv_in, 16)

        @block.tensor
        def _(pe):
            def rotate(m):
                pe.wait_ge(raw_ready, m + 1)
                if m >= 2:
                    pe.wait_ge(done, m - 1)
                nc.tensor.matmul(k.ps[:, 4 + m % 2, :], rot[:], raw[:, m % 2, :], start=True, stop=True).then_inc(rotated, 1)

            pe.wait_ge(small_in, 32)
            for m in range(NM + 1):
                if m < NM:
                    pe.wait_ge(w_in[m % RW], 16 * (m // RW + 1))
                    if m >= 2:
                        pe.wait_ge(raw_ready, m - 1)
                    for kt in range(KD):
                        mm = nc.tensor.matmul(k.ps[:, 2 * (m % 2), :], w[:, m % RW, kt * P:(kt + 1) * P], hT[:, kt, 0:TL],
                                              start=kt == 0, stop=kt == KD - 1)
                        if m >= AH:
                            mm = nc.tensor.matmul(k.ps[:, 2 * (m % 2) + 1, 0:CTX * P], w[:, m % RW, kt * P:(kt + 1) * P], hT[:, kt, TL:T],
                                                  start=kt == 0, stop=kt == KD - 1)
                    mm.then_inc(projected, 1)
                if m:
                    rotate(m - 1)
            pe.wait_ge(wv_in, 32)
            for n in range(2):
                for t in range(NT):
                    i = n * NT + t
                    if i >= 2:
                        pe.wait_ge(v_read, i - 1)
                    for kt in range(KD):
                        mm = nc.tensor.matmul(k.ps[:, 6 + i % 2, :], hT[:, kt, t * P:(t + 1) * P], wv[:, n, kt * BANK:(kt + 1) * BANK],
                                              start=kt == 0, stop=kt == KD - 1)
                    mm.then_inc(v_full, 1)

        @block.scalar
        def _(act):
            for m in range(NM):
                act.wait_ge(projected, m + 1)
                if m >= 2:
                    act.wait_ge(done, m - 1)
                if m >= AH:
                    nc.scalar.activation(kT[:, m - AH, TL:T], k.ps[:, 2 * (m % 2) + 1, 0:CTX * P], ACT.Copy)
                nc.scalar.activation(raw[:, m % 2, :], k.ps[:, 2 * (m % 2), :], ACT.Copy, scale=0.125 if m < AH else 1.0).then_inc(raw_ready, 1)
            for n in range(2):
                for t in range(NT):
                    i = n * NT + t
                    act.wait_ge(v_full, i + 1)
                    nc.scalar.activation(v[:, t, n * BANK:(n + 1) * BANK], k.ps[:, 6 + i % 2, :], ACT.Copy).then_inc(v_read, 1)

        @block.vector
        def _(dve):
            dve.wait_ge(small_in, 32)
            for m in range(NM):
                dst = qT[:, m, :] if m < AH else kT[:, m - AH, 0:TL]
                dve.wait_ge(rotated, m + 1)
                nc.vector.tensor_tensor(rs[:, m % 2, :], k.ps[:, 4 + m % 2, :], rope[:, 1, :], ALU.mult)
                nc.vector.tensor_tensor(dst, raw[:, m % 2, :], rope[:, 0, :], ALU.mult)
                dve.drain()
                nc.vector.tensor_tensor(dst, dst, rs[:, m % 2, :], ALU.add).then_inc(done, 1)


def attend_stage(k, qT, kT, v, o):
    nc, ins = k.nc, k.ins
    with ExitStack() as ctx:
        sb = sbuf(ctx, nc)
        lam = sb("at_lam", [P, 2, P])
        ls = sb("at_ls", [P, 2])
        nl = sb("at_nl", [P, 1])
        p = sb("at_p", [P, 2, 2, T])
        wT = sb("at_wT", [P, 2, T])
        nmax, tot, inv = sb("at_nmax", [P, 2, 2]), sb("at_tot", [P, 2, 2]), sb("at_inv", [P, 2, 2])
        lam_in, lam_sum, lam_exp = k.sem("at_lam_in"), k.sem("at_lam_sum"), k.sem("at_lam_exp")
        scored, maxed, exped, combined = k.sem("at_scored"), k.sem("at_maxed"), k.sem("at_exped"), k.sem("at_combined")
        turned, copied, full, read = k.sem("at_turned"), k.sem("at_copied"), k.sem("at_full"), k.sem("at_read")
        block = ctx.enter_context(nc.Block())
        N = LAT * AH

        @block.sync
        def _(sp):
            sp.dma_start(lam[:, 0, :], ins["lambda_q"].partition_broadcast(P)).then_inc(lam_in, 16)
            sp.dma_start(lam[:, 1, :], ins["lambda_k"].partition_broadcast(P)).then_inc(lam_in, 16)

        @block.tensor
        def _(pe):
            def score(n):
                t, h = n // AH, n % AH
                rows = slice(64 * (h % 2), 64 * (h % 2) + 64)
                for mp in range(2):
                    if n >= 1:
                        pe.wait_ge(exped, 2 * (n - 1) + mp + 1)
                    m = mp * 4 + h // 2
                    for o_, a, c in ((0, 0, TL), (BANK, TL, CTX * P)):
                        mm = nc.tensor.matmul(k.flat[:, mp * 2 * BANK + o_:mp * 2 * BANK + o_ + c], qT[rows, m, t * P:(t + 1) * P],
                                              kT[rows, m, a:a + c], start=True, stop=True)
                    mm.then_inc(scored, 1)

            def values(n):
                h = n % AH
                pe.wait_ge(combined, n + 1)
                if n >= 1:
                    pe.wait_ge(copied, n)
                for t in range(NT):
                    mm = nc.tensor.transpose(k.flat[:, 4 * BANK + t * P:4 * BANK + (t + 1) * P], p[:, n % 2, 0, t * P:(t + 1) * P], k.ident[:])
                mm.then_inc(turned, 1)
                pe.wait_ge(copied, n + 1)
                if n >= 2:
                    pe.wait_ge(read, n - 1)
                for t in range(NT):
                    mm = nc.tensor.matmul(k.ps[:, 6 + n % 2, 0:P], wT[:, n % 2, t * P:(t + 1) * P], v[:, t, h * AV:(h + 1) * AV],
                                          start=t == 0, stop=t == NT - 1)
                mm.then_inc(full, 1)

            for n in range(N + 1):
                if n < N:
                    score(n)
                if n:
                    values(n - 1)

        @block.scalar
        def _(act):
            act.wait_ge(lam_sum, 1)
            nc.scalar.activation(ls[:], ls[:], ACT.Exp).then_inc(lam_exp, 1)

            def tail(n):
                act.wait_ge(turned, n + 1)
                if n >= 2:
                    act.wait_ge(full, n - 1)
                nc.scalar.activation(wT[:, n % 2, :], k.flat[:, 4 * BANK:4 * BANK + T], ACT.Copy).then_inc(copied, 1)

            def read_out(n):
                act.wait_ge(full, n + 1)
                nc.scalar.activation(o[:, n // AH, (n % AH) * AV:(n % AH + 1) * AV], k.ps[:, 6 + n % 2, 0:P], ACT.Copy).then_inc(read, 1)

            for n in range(N + 2):
                if n < N:
                    if n >= 2:
                        act.wait_ge(turned, n - 1)
                    for mp in range(2):
                        act.wait_ge(maxed, 2 * n + mp + 1)
                        nc.scalar.activation(p[:, n % 2, mp, :], k.flat[:, mp * 2 * BANK:mp * 2 * BANK + T], ACT.Exp,
                                                    bias=nmax[:, n % 2, mp:mp + 1], accum_out=tot[:, n % 2, mp:mp + 1]).then_inc(exped, 1)
                if 1 <= n <= N:
                    tail(n - 1)
                if n >= 2:
                    read_out(n - 2)

        @block.vector
        def _(dve):
            V = nc.vector
            dve.wait_ge(lam_in, 32)
            V.tensor_tensor(lam[:, 0, :], lam[:, 0, :], lam[:, 1, :], ALU.mult)
            dve.drain()
            V.tensor_reduce(ls[:], lam[:, 0, :].rearrange("p (a b) -> p a b", a=2), AX.X, ALU.add).then_inc(lam_sum, 1)
            dve.wait_ge(lam_exp, 1)
            V.tensor_tensor(nl[:], ls[:, 1:2], ls[:, 0:1], ALU.subtract)
            dve.drain()
            V.tensor_scalar(nl[:], nl[:], -LAMBDA_INIT, None, ALU.add)
            dve.drain()

            def combine(n):
                s = n % 2
                dve.wait_ge(exped, 2 * n + 2)
                V.reciprocal(inv[:, s, :], tot[:, s, :])
                dve.drain()
                V.tensor_tensor(inv[:, s, 1:2], inv[:, s, 1:2], nl[:], ALU.mult)
                V.tensor_scalar(p[:, s, 0, :], p[:, s, 0, :], inv[:, s, 0:1], None, ALU.mult)
                dve.drain()
                V.scalar_tensor_tensor(out=p[:, s, 0, :], in0=p[:, s, 1, :], scalar=inv[:, s, 1:2], in1=p[:, s, 0, :],
                                       op0=ALU.mult, op1=ALU.add).then_inc(combined, 1)

            for n in range(N + 1):
                if n < N:
                    for mp in range(2):
                        dve.wait_ge(scored, 2 * n + mp + 1)
                        V.tensor_reduce(nmax[:, n % 2, mp:mp + 1], k.flat[:, mp * 2 * BANK:mp * 2 * BANK + T], AX.X, ALU.max,
                                        negate=True).then_inc(maxed, 1)
                if n:
                    combine(n - 1)


def attention_output_stage(k, o, src, dst):
    nc, ins = k.nc, k.ins
    with ExitStack() as ctx:
        sb = sbuf(ctx, nc)
        w = sb("ao_w", [P, AH, D])
        sg = sb("ao_sg", [P, 1])
        gate = sb("ao_gate", [P, D])
        x = sb("ao_x", [P, LAT, D])
        sq = sb("ao_sq", [P, D])
        ss = sb("ao_ss", [P, LAT, AH])
        oT = sb("ao_oT", [P, AH, P])
        w_in, small_in, x_in = k.sem("ao_w_in"), k.sem("ao_small_in"), k.sem("ao_x_in")
        mean, root, normed, turned, copied = k.sem("ao_mean"), k.sem("ao_root"), k.sem("ao_normed"), k.sem("ao_turned"), k.sem("ao_copied")
        full, added, stored, scaled = k.sem("ao_full"), k.sem("ao_added"), k.sem("ao_stored"), k.sem("ao_scaled")
        block = ctx.enter_context(nc.Block())
        heads = lambda a: a.rearrange("p (h e) -> p h e", h=AH)

        @block.sync
        def _(sp):
            sp.dma_start(w[:], ins["attn_out_w"]).then_inc(w_in, 16)
            sp.dma_start(sg[:], ins["subln_g"]).then_inc(small_in, 16)
            sp.dma_start(gate[:], k.mods[1, 0, 2 * D:3 * D].partition_broadcast(P)).then_inc(small_in, 16)
            for t in range(LAT):
                sp.dma_start(x[:, t, :], src[t]).then_inc(x_in, 16)
            for t in range(LAT):
                sp.wait_ge(added, t + 1)
                sp.dma_start(dst[t], x[:, t, :]).then_inc(stored, 16)
            sp.wait_ge(stored, 16 * LAT)

        @block.scalar
        def _(act):
            act.wait_ge(mean, 1)
            nc.scalar.activation(ss[:], ss[:], ACT.Sqrt).then_inc(root, 1)
            act.wait_ge(scaled, 1)
            for t in range(LAT):
                for h in range(AH):
                    n = t * AH + h
                    act.wait_ge(turned, n + 1)
                    nc.scalar.activation(oT[:, h, :], k.ps[:, n % 4, 0:P], ACT.Copy, scale=sg[:, 0:1]).then_inc(copied, 1)

        @block.vector
        def _(dve):
            V = nc.vector
            dve.wait_ge(small_in, 32)
            V.tensor_scalar(sg[:], sg[:], 1.0 - LAMBDA_INIT, None, ALU.mult).then_inc(scaled, 1)
            for t in range(LAT):
                dve.drain()
                V.tensor_tensor(sq[:], o[:, t, :], o[:, t, :], ALU.mult)
                dve.drain()
                V.tensor_reduce(ss[:, t, :], heads(sq[:]), AX.X, ALU.add)
            dve.drain()
            V.tensor_scalar(ss[:], ss[:], 1.0 / AV, EPS, ALU.mult, ALU.add).then_inc(mean, 1)
            dve.wait_ge(root, 1)
            V.reciprocal(ss[:], ss[:])
            dve.drain()
            for t in range(LAT):
                V.tensor_tensor(heads(o[:, t, :]), heads(o[:, t, :]), bcast(ss[:, t, :].unsqueeze(2), [P, AH, AV]), ALU.mult).then_inc(normed, 1)
            dve.wait_ge(x_in, 16 * LAT)
            for t in range(LAT):
                b = 4 + 2 * (t % 2)
                dve.wait_ge(full, t + 1)
                V.tensor_tensor(sq[:], k.flat[:, b * BANK:(b + 2) * BANK], gate[:], ALU.mult)
                dve.drain()
                V.tensor_tensor(x[:, t, :], x[:, t, :], sq[:], ALU.add).then_inc(added, 1)
                dve.drain()

        @block.tensor
        def _(pe):
            for t in range(LAT):
                pe.wait_ge(normed, t + 1)
                for h in range(AH):
                    n = t * AH + h
                    if n >= 4:
                        pe.wait_ge(copied, n - 3)
                    nc.tensor.transpose(k.ps[:, n % 4, 0:P], o[:, t, h * AV:(h + 1) * AV], k.ident[:]).then_inc(turned, 1)
                if t == 0:
                    pe.wait_ge(w_in, 16)
                if t >= 2:
                    pe.wait_ge(added, t - 1)
                pe.wait_ge(copied, (t + 1) * AH)
                b = 4 + 2 * (t % 2)
                for n in range(2):
                    for h in range(AH):
                        mm = nc.tensor.matmul(k.ps[:, b + n, :], oT[:, h, :], w[:, h, n * BANK:(n + 1) * BANK], start=h == 0, stop=h == AH - 1)
                mm.then_inc(full, 1)


def final_stage(k, src, out):
    nc, ins = k.nc, k.ins
    with ExitStack() as ctx:
        sb = sbuf(ctx, nc)
        x = sb("fi_x", [P, LAT, D])
        g = sb("fi_g", [P, D])
        sq = sb("fi_sq", [P, D])
        ss = sb("fi_ss", [P, LAT])
        g_in, squared, mean, root, ready, stored = (k.sem("fi_g_in"), k.sem("fi_squared"), k.sem("fi_mean"), k.sem("fi_root"),
                                                   k.sem("fi_ready"), k.sem("fi_stored"))
        x_in = [k.sem(f"fi_x_in{t}") for t in range(LAT)]
        block = ctx.enter_context(nc.Block())

        @block.sync
        def _(sp):
            for t in range(LAT):
                sp.dma_start(x[:, t, :], src[t]).then_inc(x_in[t], 16)
            sp.dma_start(g[:], ins["final_norm_g"].partition_broadcast(P)).then_inc(g_in, 16)
            for t in range(LAT):
                sp.wait_ge(ready, t + 1)
                sp.dma_start(out[0, t * P:(t + 1) * P, :], x[:, t, :]).then_inc(stored, 16)
            sp.wait_ge(stored, 16 * LAT)

        @block.scalar
        def _(act):
            for t in range(LAT):
                act.wait_ge(x_in[t], 16)
                if t:
                    act.wait_ge(squared, t)
                nc.scalar.activation(sq[:], x[:, t, :], ACT.Square, accum_out=ss[:, t:t + 1]).then_inc(squared, 1)
            act.wait_ge(mean, 1)
            nc.scalar.activation(ss[:], ss[:], ACT.Sqrt).then_inc(root, 1)

        @block.vector
        def _(dve):
            dve.wait_ge(squared, LAT)
            nc.vector.tensor_scalar(ss[:], ss[:], 1.0 / D, EPS, ALU.mult, ALU.add).then_inc(mean, 1)
            dve.wait_ge(root, 1)
            nc.vector.reciprocal(ss[:], ss[:])
            dve.wait_ge(g_in, 16)
            dve.drain()
            for t in range(LAT):
                nc.vector.scalar_tensor_tensor(out=x[:, t, :], in0=x[:, t, :], scalar=ss[:, t:t + 1], in1=g[:],
                                               op0=ALU.mult, op1=ALU.mult).then_inc(ready, 1)


def build(nc, ins, out, debug=False, upto=99):
    with ExitStack() as top:
        k = Core(nc, top, ins, debug)
        sb = sbuf(top, nc)
        ident, tri, ones = sb("ident", [P, P]), sb("tri", [P, 2, P]), sb("ones", [P, P])
        k.ident, k.tri, k.ones = ident, tri, ones
        const_in = k.sem("const_in")
        with nc.Block() as block:
            @block.sync
            def _(sp):
                sp.dma_start(ident[:], ins["ident"]).then_inc(const_in, 16)
                sp.dma_start(tri[:], ins["tri"]).then_inc(const_in, 16)
                sp.dma_start(ones[:], ins["ones"]).then_inc(const_in, 16)
                sp.wait_ge(const_in, 48)
        k.end_stage()
        modulation_stage(k)
        k.end_stage()
        x1, x2, x3, x4 = k.xs
        with ExitStack() as ctx:
            wide = sbuf(ctx, nc)("y", [P, NT, DI])
            flat = wide[:].rearrange("p t c -> p (t c)")
            hT = flat[:, 0:KD * T].rearrange("p (k c) -> p k c", k=KD)
            w = flat[:, KD * T:KD * T + 4 * KD * P].rearrange("p (s c) -> p s c", s=4)
            norm_stage(k, ins["x_all"], 0, ins["norm_mix_g"][0], 0, 1, NT, hT, False)
            k.end_stage()
            with ExitStack() as scan:
                s2 = sbuf(scan, nc)
                xb, bct, dt = s2("xb", [P, NT, DI + MB * P]), s2("bct", [P, 2 * MB, T]), s2("dt", [P, NT, DH])
                ssd_project_stage(k, hT, w, xb, bct, dt)
                k.end_stage()
                ssd_scan_stage(k, xb, bct, dt, wide)
                k.end_stage()
            ssd_output_stage(k, wide, ins["x_all"], x1)
            k.end_stage()
        for layer in range(2):
            tiles = NT if layer == 0 else LAT
            src, dst = (x1, x2) if layer == 0 else (x3, x4)
            if layer == 1:
                with ExitStack() as ctx:
                    s2 = sbuf(ctx, nc)
                    o, qT, kT, v = s2("o", [P, LAT, D]), s2("qT", [P, AH, TL]), s2("kT", [P, AH, T]), s2("v", [P, NT, D])
                    with ExitStack() as c2:
                        hT = sbuf(c2, nc)("hT_a", [P, KD, T])
                        norm_stage(k, x2, 1, ins["norm_mix_g"][1], 0, 1, NT, hT, False)
                        k.end_stage()
                        attention_project_stage(k, hT, qT, kT, v)
                        k.end_stage()
                    attend_stage(k, qT, kT, v, o)
                    k.end_stage()
                    attention_output_stage(k, o, x2, x3)
                    k.end_stage()
            with ExitStack() as ctx:
                s2 = sbuf(ctx, nc)
                ids, gates = s2(f"ids{layer}", [P, NT, PH, TOPK], U32), s2(f"gates{layer}", [P, NT, PH, TOPK])
                with ExitStack() as c2:
                    hT = sbuf(c2, nc)(f"hT_p{layer}", [P, KD, T])
                    norm_stage(k, src, layer, ins["norm_ffn_g"][layer], 3, 4, tiles, hT, True)
                    k.end_stage()
                    select_stage(k, layer, tiles, hT, ids, gates)
                    k.end_stage()
                expert_stage(k, layer, tiles, ids, gates, src, dst)
                k.end_stage()
        final_stage(k, x4, out)
        k.end_stage()


def lay_out(inputs):
    f = lambda n: np.asarray(inputs[n])
    cut = lambda w, n: np.ascontiguousarray(w.reshape(w.shape[0] // P, P, w.shape[1] // n, n).transpose(2, 1, 0, 3)).reshape(
        w.shape[1] // n, P, -1)
    cols = lambda v: np.ascontiguousarray(v.reshape(-1, P).T)
    a = {}
    a["x_all"] = np.concatenate([f("x")[0], f("ctx")[0]]).reshape(NT, P, D)
    a["c_cols"] = np.ascontiguousarray(np.stack([f("c")[0], f("c_ctx")]).reshape(2, KD, P).transpose(2, 1, 0))
    a["ada_w"] = np.concatenate([cut(f("ada_w")[l], BANK) for l in range(2)])
    a["ada_b"] = f("ada_b").reshape(1, -1)
    in_w = f("ssd_in_w")[0]
    a["w_z"] = cut(in_w[:, 0:DI], BANK)
    a["w_xbc"] = cut(in_w[:, DI:2 * DI + 2 * MB * P], P)
    a["w_dt"] = cut(in_w[:, 2 * DI + 2 * MB * P:], DH)[0]
    a["conv_w"] = np.ascontiguousarray(f("ssd_conv_w")[0].reshape(5, -1, P).transpose(2, 1, 0))
    a["conv_b"] = cols(f("ssd_conv_b")[0])
    a["dt_bias"], a["a_log"], a["ssd_d"] = (f(n)[0].reshape(-1) for n in ("ssd_dt_bias", "ssd_a_log", "ssd_d"))
    a["ssd_norm_g"] = cols(f("ssd_norm_g")[0])
    a["ssd_out_w"] = np.ascontiguousarray(f("ssd_out_w")[0].reshape(MX, P, D).transpose(1, 0, 2))
    a["norm_mix_g"], a["norm_ffn_g"], a["final_norm_g"] = f("norm_mix_g"), f("norm_ffn_g"), f("final_norm_g")
    qkv = f("attn_qkv_w")[0]
    a["w_qk"], a["w_v"] = cut(qkv[:, 0:2 * D], P), cut(qkv[:, 2 * D:], BANK)
    a["lambda_q"], a["lambda_k"] = f("attn_lambda_q")[0].reshape(-1), f("attn_lambda_k")[0].reshape(-1)
    a["subln_g"] = f("attn_subln_g")[0].reshape(P, 1)
    a["attn_out_w"] = np.ascontiguousarray(f("attn_out_w")[0].reshape(AH, P, D).transpose(1, 0, 2))
    a["peer_q_w"] = np.stack([cut(f("peer_q_w")[l], P) for l in range(2)])
    a["peer_keys"] = np.ascontiguousarray(f("peer_keys").reshape(2, HC, NKEYS, P).transpose(0, 3, 1, 2))
    for l in range(2):
        a[f"peer_uv{l}"] = np.concatenate([f("peer_u")[l], f("peer_v")[l]], axis=1)
    j, i = np.arange(P)[:, None], np.arange(P)[None, :]
    a["ident"] = np.eye(P, dtype=np.float32)
    a["ones"] = np.ones((P, P), np.float32)
    a["tri"] = np.stack([j <= i, j >= i], axis=1).astype(np.float32)
    a["iota"] = np.arange(TOPK, dtype=np.float32)
    tok = np.arange(TL)
    freq = np.float32(10000.0) ** (-np.arange(0, 32, 2, dtype=np.float32) / np.float32(32))
    row, col = (tok // 64).astype(np.float32)[:, None] * freq, (tok % 64).astype(np.float32)[:, None] * freq
    ang = np.concatenate([row, row, col, col], axis=1).astype(np.float32)
    ang = np.concatenate([ang, ang], axis=1).T
    a["rope"] = np.ascontiguousarray(np.stack([np.cos(ang), np.sin(ang)], axis=1)).astype(np.float32)
    rot = np.zeros((P, P), np.float32)
    for c in range(P):
        if c % 32 < 16:
            rot[c + 16, c] = -1.0
        else:
            rot[c - 16, c] = 1.0
    a["rot"] = rot
    return a


def kernel(**inputs):
    import concourse.bacc as bacc
    from concourse.bass_utils import run_bass_kernel_spmd as run

    nc = bacc.Bacc("TRN2", target_bir_lowering=False, num_devices=1)
    arrays = lay_out(inputs)
    ins = {n: nc.dram_tensor(f"in_{n}", a.shape, mybir.dt.from_np(a.dtype), kind="ExternalInput").ap() for n, a in arrays.items()}
    out = nc.dram_tensor("out", (1, TL, D), F32, kind="ExternalOutput").ap()
    build(nc, ins, out)
    r = run(nc, [{f"in_{n}": a for n, a in arrays.items()}], core_ids=[0])
    return r.results[0]["out"]
```

```python
from contextlib import ExitStack
import math

import numpy as np
import concourse.bass as bass
from concourse import mybir

ALU = mybir.AluOpType
ACT = mybir.ActivationFunctionType
AX = mybir.AxisListType
F32 = mybir.dt.float32
U32 = mybir.dt.uint32

P = 128
D = 1024
KD = D // P
LAT, CTX = 4, 2
NT = LAT + CTX
T = NT * P
TL = LAT * P
EPS = 1e-6
BANK = 512

DI = 2048
MX, MB = DI // P, 4
HEADS, GROUPS, HPG, HD = 32, 4, 8, 64
DH = 2 * HEADS

AH, AV = 8, 128
LAMBDA_INIT = 0.8 - 0.6 * math.exp(-0.3)

PH, TOPK, NKEYS = 8, 16, 128
HC = 2 * PH
SLOTS = 8
NEG = -3.0e38


def bcast(ap, shape):
    return ap.broadcast_to(shape)


class Core:

    def __init__(self, nc, ctx, ins, debug):
        self.nc, self.ctx, self.ins = nc, ctx, ins
        self.names, self.stage_sems = {}, []
        self.ps = ctx.enter_context(nc.psum_tensor("ps", [P, 8, BANK], F32))
        self.flat = self.ps[:].rearrange("p b n -> p (b n)")
        kind = "ExternalOutput" if debug else "Internal"
        scratch = lambda name, shape: nc.dram_tensor(name, shape, F32, kind=kind).ap()
        self.mods = scratch("mods", [2, NT, 6 * D])
        self.h = scratch("h_scratch", [NT, P, D])
        self.z = scratch("z_scratch", [4, NT, P, BANK])
        self.xs = [scratch(f"x_scratch{i}", [NT, P, D]) for i in range(4)]
        self.passed = {e: self.sem(f"{e}_passed") for e in ("pe", "dve", "act", "pool", "sp")}
        self.stage_sems = []

    def sem(self, name):
        n = self.names[name] = self.names.get(name, -1) + 1
        handle = self.nc.alloc_semaphore(name=f"{name}_{n}")
        self.stage_sems.append(handle)
        return handle

    def end_stage(self):
        self.nc.clear_and_free_semaphores(self.stage_sems)
        self.nc.all_engine_barrier()
        self.stage_sems = []

    def hold(self, engine, who, sem, value):
        engine.wait_ge(sem, value)
        engine.sem_inc(self.passed[who], 1)


def sbuf(ctx, nc):
    def allocate(name, shape, dt=F32):
        return ctx.enter_context(nc.sbuf_tensor(f"{name}_{nc.next_id()}", shape, dt))
    return allocate


def modulation_stage(k):
    nc, ins = k.nc, k.ins
    CH, RING = 12, 3
    with ExitStack() as ctx:
        sb = sbuf(ctx, nc)
        c = sb("ada_c", [P, KD, 2])
        cs = sb("ada_silu", [P, KD, 2])
        w = sb("ada_w", [P, RING, KD * BANK])
        bias = sb("ada_bias", [2, 2 * 6 * D])
        m = sb("ada_m", [2, 2 * 6 * D])
        c_in, b_in, silu = k.sem("c_in"), k.sem("b_in"), k.sem("silu")
        w_in = [k.sem(f"ada_w_in{s}") for s in range(RING)]
        w_free, ps_full, ps_free = k.sem("ada_w_free"), k.sem("ada_ps_full"), k.sem("ada_ps_free")
        done = k.sem("ada_done")
        block = ctx.enter_context(nc.Block())

        @block.sync
        def _(sp):
            sp.dma_start(c[:], ins["c_cols"]).then_inc(c_in, 16)
            for r in range(2):
                sp.dma_start(bias[r:r + 1, :], ins["ada_b"]).then_inc(b_in, 16)
            with sp.Fori(0, 2 * CH // RING) as i:
                for s in range(RING):
                    sp.wait_ge(w_free, i * RING + s + 1)
                    sp.dma_start(w[:, s, :], ins["ada_w"][bass.ds(i * RING + s, 1)].rearrange(
                        "o p n -> (o p) n")).then_inc(w_in[s], 16)
            sp.wait_ge(ps_free, RING + 2 * CH)
            for l in range(2):
                for t in range(NT):
                    r = 0 if t < LAT else 1
                    sp.dma_start(k.mods[l, t:t + 1, :], m[r:r + 1, l * 6 * D:(l + 1) * 6 * D]).then_inc(done, 16)
            sp.wait_ge(done, 16 * 2 * NT)

        @block.scalar
        def _(act):
            act.wait_ge(c_in, 16)
            nc.scalar.activation(cs[:], c[:], ACT.Silu).then_inc(silu, 1)

        @block.tensor
        def _(pe):
            pe.sem_inc(w_free, RING)
            pe.wait_ge(silu, 1)
            with pe.Fori(0, 2 * CH // RING) as i:
                for s in range(RING):
                    pe.wait_ge(w_in[s], (i + 1) * 16)
                    k.hold(pe, "pe", ps_free, i * RING + s + 1)
                    for kt in range(KD):
                        mm = nc.tensor.matmul(k.ps[0:2, s, :], cs[:, kt, :], w[:, s, kt * BANK:(kt + 1) * BANK],
                                              start=kt == 0, stop=kt == KD - 1)
                    mm.then_inc(ps_full, 1)

        @block.vector
        def _(dve):
            dve.sem_inc(ps_free, RING)
            dve.wait_ge(b_in, 32)
            with dve.Fori(0, 2 * CH // RING) as i:
                for s in range(RING):
                    k.hold(dve, "dve", ps_full, i * RING + s + 1)
                    at = bass.ds((i * RING + s) * BANK, BANK)
                    nc.vector.tensor_tensor(m[:, at], k.ps[0:2, s, :], bias[:, at], ALU.add).then_inc(ps_free, 1)
                    dve.sem_inc(w_free, 1)


def norm_stage(k, src, layer, gain, shift_at, scale_at, tiles, hT, keep_h, ahead=()):
    nc, ins = k.nc, k.ins
    with ExitStack() as ctx:
        sb = sbuf(ctx, nc)
        x = sb("n_x", [P, NT, D])
        sq = sb("n_sq", [P, D])
        g = sb("n_g", [P, D])
        sh = sb("n_sh", [P, 2, D])
        sc = sb("n_sc", [P, 2, D])
        ss = sb("n_ss", [P, NT])
        sd = sb("n_sd", [P, NT])
        rs = sb("n_rs", [P, NT])
        x_in = [k.sem(f"n_x_in{t}") for t in range(tiles)]
        mod_in = [k.sem(f"n_mod_in{r}") for r in range(2)]
        squared, var, root, h_ready = (k.sem("n_squared"), k.sem("n_var"), k.sem("n_root"), k.sem("n_h_ready"))
        turned, copied, stored, ahead_in = k.sem("n_turned"), k.sem("n_copied"), k.sem("n_stored"), k.sem("n_ahead_in")
        block = ctx.enter_context(nc.Block())

        @block.sync
        def _(sp):
            def load_mods(r):
                for dst, at in ((sc, scale_at), (sh, shift_at)):
                    sp.dma_start(dst[:, r, :], k.mods[layer, r * LAT, at * D:(at + 1) * D].partition_broadcast(P)).then_inc(mod_in[r], 16)

            for t in range(tiles):
                sp.dma_start(x[:, t, :], src[t]).then_inc(x_in[t], 16)
                if t == 0:
                    sp.dma_start(g[:], gain.partition_broadcast(P)).then_inc(mod_in[0], 16)
                    load_mods(0)
            if tiles > LAT:
                load_mods(1)
            for to, dram in ahead:
                sp.dma_start(to, dram).then_inc(ahead_in, 16)
            if keep_h:
                for t in range(tiles):
                    sp.wait_ge(h_ready, t + 1)
                    sp.dma_start(k.h[t], x[:, t, :]).then_inc(stored, 16)
                sp.wait_ge(stored, 16 * tiles)
            if ahead:
                sp.wait_ge(ahead_in, 16 * len(ahead))

        @block.scalar
        def _(act):
            for t in range(tiles + 1):
                if t < tiles:
                    act.wait_ge(x_in[t], 16)
                    if t:
                        act.wait_ge(squared, t)
                    nc.scalar.activation(sq[:], x[:, t, :], ACT.Square, accum_out=ss[:, t:t + 1]).then_inc(squared, 1)
                if t:
                    act.wait_ge(var, t)
                    nc.scalar.activation(sd[:, t - 1:t], sd[:, t - 1:t], ACT.Sqrt).then_inc(root, 1)
            for t in range(tiles):
                act.wait_ge(turned, t + 1)
                b = 2 * (t % 2)
                nc.scalar.activation(hT[:, :, t * P:(t + 1) * P],
                                     k.flat[:, b * BANK:(b + 2) * BANK].rearrange("p (k c) -> p k c", k=KD),
                                     ACT.Copy).then_inc(copied, 1)

        @block.vector
        def _(dve):
            V = nc.vector

            def mean(t):
                dve.wait_ge(squared, t + 1)
                V.tensor_scalar(sd[:, t:t + 1], ss[:, t:t + 1], 1.0 / D, EPS, ALU.mult, ALU.add).then_inc(var, 1)

            def scales(r):
                dve.wait_ge(mod_in[r], 16 * (3 - r))
                V.scalar_tensor_tensor(out=sc[:, r, :], in0=sc[:, r, :], scalar=1.0, in1=g[:], op0=ALU.add, op1=ALU.mult)

            mean(0)
            scales(0)
            for t in range(tiles):
                r = t // LAT
                if t == LAT:
                    scales(1)
                if t + 1 < tiles:
                    mean(t + 1)
                dve.wait_ge(root, t + 1)
                V.reciprocal(rs[:, t:t + 1], sd[:, t:t + 1])
                dve.drain()
                V.scalar_tensor_tensor(out=x[:, t, :], in0=x[:, t, :], scalar=rs[:, t:t + 1], in1=sc[:, r, :], op0=ALU.mult, op1=ALU.mult)
                dve.drain()
                V.tensor_tensor(x[:, t, :], x[:, t, :], sh[:, r, :], ALU.add).then_inc(h_ready, 1)

        @block.tensor
        def _(pe):
            for t in range(tiles):
                pe.wait_ge(h_ready, t + 1)
                if t >= 2:
                    pe.wait_ge(copied, t - 1)
                b = 2 * (t % 2) * BANK
                for kt in range(KD):
                    mm = nc.tensor.transpose(k.flat[:, b + kt * P:b + (kt + 1) * P], x[:, t, kt * P:(kt + 1) * P], k.ident[:])
                mm.then_inc(turned, 1)


def ssd_project_stage(k, hT, w, xb, bct, dt):
    nc, ins = k.nc, k.ins
    PADL = TL + 4
    STRIP = PADL + CTX * P + 4
    OUT = STRIP - 4
    NM, RW = MX + 2 * MB, 4
    TURN = MX + MB
    with ExitStack() as ctx:
        sb = sbuf(ctx, nc)
        wz = sb("ip_wz", [P, 2, KD * BANK])
        wdt = sb("ip_wdt", [P, KD * DH])
        dtb = sb("ip_dtb", [P, DH])
        cw = sb("ip_cw", [P, NM, 5])
        cb = sb("ip_cb", [P, NM])
        pad = sb("ip_pad", [P, 2, STRIP])
        acc = sb("ip_acc", [P, 2, OUT])
        st = sb("ip_st", [P, 2, OUT])
        zs = sb("ip_zs", [P, 2, BANK])
        w_in = [k.sem(f"ip_w_in{s}") for s in range(RW)]
        z_in = [k.sem(f"ip_z_in{s}") for s in range(2)]
        small_in, zeroed = k.sem("ip_small_in"), k.sem("ip_zeroed")
        projected, padded, conved = k.sem("ip_projected"), k.sem("ip_padded"), k.sem("ip_conved")
        activated, turned, kept, turn_read = k.sem("ip_activated"), k.sem("ip_turned"), k.sem("ip_kept"), k.sem("ip_turn_read")
        dt_full, z_full, zs_ready = k.sem("ip_dt_full"), k.sem("ip_z_full"), k.sem("ip_zs_ready")
        z_stored = [k.sem(f"ip_z_stored{q}") for q in range(2)]
        block = ctx.enter_context(nc.Block())

        @block.sync
        def _(sp):
            for m in range(NM):
                if m >= RW:
                    sp.wait_ge(projected, m - RW + 1)
                sp.dma_start(w[:, m % RW, :], ins["w_xbc"][m]).then_inc(w_in[m % RW], 16)
                if m == 1:
                    sp.dma_start(cw[:], ins["conv_w"]).then_inc(small_in, 16)
                    sp.dma_start(cb[:], ins["conv_b"]).then_inc(small_in, 16)
                    sp.dma_start(wdt[:], ins["w_dt"]).then_inc(small_in, 16)
                    sp.dma_start(dtb[:], ins["dt_bias"].partition_broadcast(P)).then_inc(small_in, 16)
            for n in range(4):
                if n >= 2:
                    sp.wait_ge(z_full, (n - 1) * NT)
                sp.dma_start(wz[:, n % 2, :], ins["w_z"][n]).then_inc(z_in[n % 2], 16)
                for t in range(NT):
                    if n >= 1:
                        i = (n - 1) * NT + t
                        sp.wait_ge(zs_ready, i + 1)
                        sp.dma_start(k.z[n - 1, t], zs[:, i % 2, :]).then_inc(z_stored[i % 2], 16)
            for t in range(NT):
                i = 3 * NT + t
                sp.wait_ge(zs_ready, i + 1)
                sp.dma_start(k.z[3, t], zs[:, i % 2, :]).then_inc(z_stored[i % 2], 16)
            for q in range(2):
                sp.wait_ge(z_stored[q], 16 * 2 * NT)

        @block.tensor
        def _(pe):
            def turn(m):
                pe.wait_ge(activated, m + 1)
                if m >= 2:
                    pe.wait_ge(turn_read, m - 1)
                o = (4 + 2 * (m % 2)) * BANK
                for t in range(NT):
                    a = t * P if t < LAT else PADL + (t - LAT) * P
                    mm = nc.tensor.transpose(k.flat[:, o + t * P:o + (t + 1) * P], st[:, m % 2, a:a + P], k.ident[:])
                mm.then_inc(turned, 1)

            for m in range(NM):
                s = m % 2
                pe.wait_ge(w_in[m % RW], 16 * (m // RW + 1))
                if m >= 2:
                    pe.wait_ge(padded, m - 1)
                for kt in range(KD):
                    for o, a, n in ((0, 0, TL), (BANK, TL, CTX * P)):
                        mm = nc.tensor.matmul(k.flat[:, s * 2 * BANK + o:s * 2 * BANK + o + n], w[:, m % RW, kt * P:(kt + 1) * P],
                                              hT[:, kt, a:a + n], start=kt == 0, stop=kt == KD - 1)
                mm.then_inc(projected, 1)
                if 2 <= m <= TURN + 1:
                    turn(m - 2)
            pe.wait_ge(padded, NM)
            pe.wait_ge(small_in, 64)
            for t in range(NT):
                for kt in range(KD):
                    mm = nc.tensor.matmul(k.flat[:, t * DH:(t + 1) * DH], hT[:, kt, t * P:(t + 1) * P], wdt[:, kt * DH:(kt + 1) * DH],
                                          start=kt == 0, stop=kt == KD - 1)
            mm.then_inc(dt_full, 1)
            for n in range(4):
                pe.wait_ge(z_in[n % 2], 16 * (n // 2 + 1))
                for t in range(NT):
                    i = n * NT + t
                    if i >= 2:
                        pe.wait_ge(zs_ready, i - 1)
                    for kt in range(KD):
                        mm = nc.tensor.matmul(k.ps[:, 2 + i % 2, :], hT[:, kt, t * P:(t + 1) * P], wz[:, n % 2, kt * BANK:(kt + 1) * BANK],
                                              start=kt == 0, stop=kt == KD - 1)
                    mm.then_inc(z_full, 1)

        @block.scalar
        def _(act):
            def place(m):
                s = m % 2
                act.wait_ge(projected, m + 1)
                if m >= 2:
                    act.wait_ge(conved, m - 1)
                nc.scalar.activation(pad[:, s, 2:2 + TL], k.flat[:, s * 2 * BANK:s * 2 * BANK + TL], ACT.Copy)
                nc.scalar.activation(pad[:, s, PADL + 2:PADL + 2 + CTX * P],
                                     k.flat[:, (s * 2 + 1) * BANK:(s * 2 + 1) * BANK + CTX * P], ACT.Copy).then_inc(padded, 1)

            def activate(m):
                act.wait_ge(conved, m + 1)
                if m >= 2:
                    if m - 2 < TURN:
                        act.wait_ge(turned, m - 1)
                    if m - 2 >= MX:
                        act.wait_ge(kept, m - 2 - MX + 1)
                nc.scalar.activation(st[:, m % 2, :], acc[:, m % 2, :], ACT.Silu).then_inc(activated, 1)

            def read_turned(m):
                act.wait_ge(turned, m + 1)
                o = (4 + 2 * (m % 2)) * BANK
                nc.scalar.activation(xb[:, :, m * P:(m + 1) * P], k.flat[:, o:o + T].rearrange("p (t c) -> p t c", t=NT),
                                     ACT.Copy).then_inc(turn_read, 1)

            act.wait_ge(zeroed, 1)
            for m in range(NM + 2):
                if m < NM:
                    place(m)
                if 1 <= m <= NM:
                    activate(m - 1)
                if 2 <= m <= TURN + 1:
                    read_turned(m - 2)
            for i in range(4 * NT):
                act.wait_ge(z_full, i + 1)
                if i >= 2:
                    act.wait_ge(z_stored[i % 2], 16 * (i // 2))
                nc.scalar.activation(zs[:, i % 2, :], k.ps[:, 2 + i % 2, :], ACT.Silu).then_inc(zs_ready, 1)

        @block.vector
        def _(dve):
            nc.vector.memset(pad[:], 0.0).then_inc(zeroed, 1)
            dve.wait_ge(small_in, 64)
            for m in range(NM):
                s = m % 2
                dve.wait_ge(padded, m + 1)
                if m >= 2:
                    dve.wait_ge(activated, m - 1)
                nc.vector.tensor_scalar(acc[:, s, :], pad[:, s, 0:OUT], cw[:, m, 0:1], cb[:, m:m + 1], ALU.mult, ALU.add)
                for tap in range(1, 5):
                    dve.drain()
                    last = nc.vector.scalar_tensor_tensor(out=acc[:, s, :], in0=pad[:, s, tap:tap + OUT], scalar=cw[:, m, tap:tap + 1],
                                                          in1=acc[:, s, :], op0=ALU.mult, op1=ALU.add)
                last.then_inc(conved, 1)
            dve.wait_ge(dt_full, 1)
            nc.vector.tensor_tensor(dt[:], k.flat[:, 0:NT * DH].rearrange("p (t c) -> p t c", t=NT),
                                    bcast(dtb[:].unsqueeze(1), [P, NT, DH]), ALU.add)

        @block.gpsimd
        def _(pool):
            for m in range(MX, NM):
                pool.wait_ge(activated, m + 1)
                nc.gpsimd.tensor_copy(bct[:, m - MX, 0:TL], st[:, m % 2, 0:TL])
                nc.gpsimd.tensor_copy(bct[:, m - MX, TL:T], st[:, m % 2, PADL:PADL + CTX * P]).then_inc(kept, 1)


def ssd_scan_stage(k, xb, bct, dt, y):
    nc, ins = k.nc, k.ins
    AHEAD = 2
    WS = 2 * (AHEAD + 1)
    with ExitStack() as ctx:
        sb = sbuf(ctx, nc)
        a = sb("sc_a", [P, DH])
        dsk = sb("sc_d", [P, DH])
        tmp = [sb(f"sc_tmp{i}", [P, NT * DH]) for i in range(3)]
        dta = sb("sc_dta", [P, NT, DH])
        cs = sb("sc_cs", [P, NT, DH])
        ncs = sb("sc_ncs", [P, NT, DH])
        ecs = sb("sc_ecs", [P, NT, DH])
        etot = sb("sc_etot", [P, NT, DH])
        wend = sb("sc_wend", [P, NT, DH])
        dsum = sb("sc_dsum", [P, HEADS])
        state = sb("sc_state", [P, DI])
        xdt = sb("sc_xdt", [P, 2, DI])
        xw = sb("sc_xw", [P, DI])
        cbm = sb("sc_cbm", [P, AHEAD + 1, P])
        seg = sb("sc_seg", [P, 4, BANK])
        w = sb("sc_w", [P, WS, BANK])
        off = sb("sc_off", [P, BANK])
        small_in = k.sem("sc_small_in")
        pre = {n: k.sem(f"sc_{n}") for n in ("decay", "absolute", "exped", "dta", "sums", "cs", "ecs", "ready", "y0")}
        xdt_ready, xw_ready, zero_state = k.sem("sc_xdt_ready"), k.sem("sc_xw_ready"), k.sem("sc_zero_state")
        cb_full, cb_masked = k.sem("sc_cb_full"), k.sem("sc_cb_masked")
        row_full, clamped, exped, weighed = k.sem("sc_row_full"), k.sem("sc_clamped"), k.sem("sc_exped"), k.sem("sc_weighed")
        y_full, y_read, s_full, s_read = k.sem("sc_y_full"), k.sem("sc_y_read"), k.sem("sc_s_full"), k.sem("sc_s_read")
        off_full, off_read = k.sem("sc_off_full"), k.sem("sc_off_read")
        block = ctx.enter_context(nc.Block())
        steps = [(0, c) for c in (4, 5, 0, 1, 2, 3)] + [(1, c) for c in (5, 4, 3, 2, 1, 0)]
        NS = len(steps)
        NG = NS * GROUPS
        flat = lambda t: t[:].rearrange("p t c -> p (t c)")

        @block.sync
        def _(sp):
            sp.dma_start(a[:], ins["a_log"].partition_broadcast(P)).then_inc(small_in, 16)
            sp.dma_start(dsk[:], ins["ssd_d"].partition_broadcast(P)).then_inc(small_in, 16)

        @block.scalar
        def _(act):
            act.wait_ge(small_in, 32)
            nc.scalar.activation(a[:], a[:], ACT.Exp).then_inc(pre["decay"], 1)
            act.wait_ge(pre["absolute"], 1)
            nc.scalar.activation(tmp[1][:], tmp[0][:], ACT.Exp, scale=-1.0).then_inc(pre["exped"], 1)
            act.wait_ge(pre["cs"], 1)
            nc.scalar.activation(flat(ecs), flat(cs), ACT.Exp)
            nc.scalar.activation(flat(wend), flat(wend), ACT.Exp)
            nc.scalar.activation(flat(etot), flat(etot), ACT.Exp).then_inc(pre["ecs"], 1)
            for i, (d, c) in enumerate(steps):
                for q in range(2 * GROUPS):
                    n = i * 2 * GROUPS + q
                    act.wait_ge(clamped, n + 1)
                    if n >= WS:
                        act.wait_ge(y_full, (n - WS) // 2 + 1)
                    for r in range(4):
                        h = d * HEADS + q * 4 + r
                        last = nc.scalar.activation(w[:, n % WS, r * P:(r + 1) * P], seg[:, n % 4, r * P:(r + 1) * P], ACT.Exp,
                                                    bias=ncs[:, c, h:h + 1])
                    last.then_inc(exped, 1)

        @block.gpsimd
        def _(pool):
            pool.wait_ge(pre["ready"], 1)

            def start_y(i):
                c = steps[i][1]
                nc.gpsimd.tensor_tensor(y[:, c, :].rearrange("p (h e) -> p h e", h=HEADS),
                                        xb[:, c, 0:DI].rearrange("p (h e) -> p h e", h=HEADS),
                                        bcast(dsum[:].unsqueeze(2), [P, HEADS, HD]), ALU.mult).then_inc(pre["y0"], 1)

            def scale_x(i):
                d, c = steps[i]
                if i >= 2:
                    pool.wait_ge(y_full, (i - 1) * GROUPS)
                nc.gpsimd.tensor_tensor(xdt[:, i % 2, :].rearrange("p (h e) -> p h e", h=HEADS),
                                        xb[:, c, 0:DI].rearrange("p (h e) -> p h e", h=HEADS),
                                        bcast(dt[:, c, d * HEADS:(d + 1) * HEADS].unsqueeze(2), [P, HEADS, HD]),
                                        ALU.mult).then_inc(xdt_ready, 1)

            scale_x(0)
            for i, (d, c) in enumerate(steps):
                for q in range(2 * GROUPS):
                    if q == 2 and i == 0:
                        start_y(0)
                    if q == 4 and i + 1 < NT:
                        start_y(i + 1)
                    if q == 6 and i + 1 < NS:
                        scale_x(i + 1)
                    n = i * 2 * GROUPS + q
                    g = i * GROUPS + q // 2
                    pool.wait_ge(exped, n + 1)
                    pool.wait_ge(cb_masked, g + 1)
                    nc.gpsimd.tensor_tensor(w[:, n % WS, :].rearrange("p (r e) -> p r e", r=4),
                                            w[:, n % WS, :].rearrange("p (r e) -> p r e", r=4),
                                            bcast(cbm[:, g % (AHEAD + 1), :].unsqueeze(1), [P, 4, P]), ALU.mult).then_inc(weighed, 1)

        @block.tensor
        def _(pe):
            pe.wait_ge(pre["dta"], 1)
            for o, m in ((0, k.tri[:, 0, :]), (1, k.tri[:, 1, :]), (2, k.ones[:])):
                mm = nc.tensor.matmul(k.ps[:, o, 0:NT * DH], m, flat(dta), start=True, stop=True)
            mm.then_inc(pre["sums"], 1)
            pe.wait_ge(pre["ready"], 1)
            def c_b(G):
                (_, c), g = steps[G // GROUPS], G % GROUPS
                if G >= 1:
                    pe.wait_ge(cb_masked, G)
                nc.tensor.matmul(k.ps[:, 2, 0:P], bct[:, g, c * P:(c + 1) * P], bct[:, MB + g, c * P:(c + 1) * P],
                                 start=True, stop=True).then_inc(cb_full, 1)

            def rows(n):
                (d, c), g = steps[n // 2 // GROUPS], n // 2 % GROUPS
                if n >= 2:
                    pe.wait_ge(clamped, n - 1)
                for r in range(4):
                    h = d * HEADS + g * HPG + (n % 2) * 4 + r
                    mm = nc.tensor.matmul(k.ps[:, n % 2, r * P:(r + 1) * P], bcast(dta[:, c, h:h + 1], [P, P]), k.tri[:, d, :],
                                          start=True, stop=True)
                mm.then_inc(row_full, 1)

            def y_of_state(G):
                i, g = G // GROUPS, G % GROUPS
                c = steps[i][1]
                if G >= 1:
                    pe.wait_ge(off_read, G)
                if i in (0, NT):
                    pe.wait_ge(zero_state, 1 + i // NT)
                else:
                    pe.wait_ge(s_read, G - GROUPS + 1)
                nc.tensor.matmul(k.ps[:, 5, :], bct[:, MB + g, c * P:(c + 1) * P], state[:, g * BANK:(g + 1) * BANK],
                                 start=True, stop=True).then_inc(off_full, 1)

            def chunk_state(G):
                i, g = G // GROUPS, G % GROUPS
                c = steps[i][1]
                pe.wait_ge(xw_ready, i + 1)
                if G >= 2:
                    pe.wait_ge(s_read, G - 1)
                nc.tensor.matmul(k.ps[:, 6 + G % 2, :], xb[:, c, DI + g * P:DI + (g + 1) * P], xw[:, g * BANK:(g + 1) * BANK],
                                 start=True, stop=True).then_inc(s_full, 1)

            def y_of_chunk(G):
                i, g = G // GROUPS, G % GROUPS
                pe.wait_ge(xdt_ready, i + 1)
                if G >= 2:
                    pe.wait_ge(y_read, G - 1)
                for n in (2 * G, 2 * G + 1):
                    pe.wait_ge(weighed, n + 1)
                    for r in range(4):
                        e = ((n % 2) * 4 + r) * HD
                        mm = nc.tensor.matmul(k.ps[:, 3 + G % 2, e:e + HD], w[:, n % WS, r * P:(r + 1) * P],
                                              xdt[:, i % 2, g * BANK + e:g * BANK + e + HD], start=True, stop=True)
                mm.then_inc(y_full, 1)

            for F in range(NG + AHEAD):
                G = F - AHEAD
                if F < NG:
                    c_b(F)
                if G >= 0:
                    y_of_state(G)
                if F < NG:
                    rows(2 * F)
                if G >= 0:
                    chunk_state(G)
                if F < NG:
                    rows(2 * F + 1)
                if G >= 0:
                    y_of_chunk(G)

        @block.vector
        def _(dve):
            dve.wait_ge(small_in, 32)
            v = flat(dt)
            nc.vector.scalar_tensor_tensor(out=tmp[0][:], in0=v, scalar=-1.0, in1=v, op0=ALU.mult, op1=ALU.max).then_inc(pre["absolute"], 1)
            dve.wait_ge(pre["exped"], 1)
            nc.vector.tensor_scalar(tmp[2][:], tmp[1][:], 2.0, None, ALU.add)
            dve.drain()
            nc.vector.reciprocal(tmp[2][:], tmp[2][:])
            dve.drain()
            nc.vector.tensor_tensor(tmp[1][:], tmp[1][:], tmp[2][:], ALU.mult)
            dve.drain()
            nc.vector.tensor_tensor(tmp[2][:], tmp[1][:], tmp[1][:], ALU.mult)
            dve.drain()
            nc.vector.tensor_scalar(tmp[0][:], tmp[2][:], 1.0 / 17, None, ALU.mult)
            for odd in (15, 13, 11, 9, 7, 5, 3):
                dve.drain()
                nc.vector.scalar_tensor_tensor(out=tmp[0][:], in0=tmp[0][:], scalar=1.0 / odd, in1=tmp[2][:], op0=ALU.add, op1=ALU.mult)
            dve.drain()
            nc.vector.scalar_tensor_tensor(out=tmp[0][:], in0=tmp[0][:], scalar=1.0, in1=tmp[1][:], op0=ALU.add, op1=ALU.mult)
            nc.vector.tensor_scalar(tmp[2][:], v, 0.0, None, ALU.max)
            dve.drain()
            nc.vector.scalar_tensor_tensor(out=v, in0=tmp[0][:], scalar=2.0, in1=tmp[2][:], op0=ALU.mult, op1=ALU.add)
            nc.vector.tensor_tensor(dsum[:], dsk[:, 0:HEADS], dsk[:, HEADS:DH], ALU.add)
            dve.wait_ge(pre["decay"], 1)
            dve.drain()
            nc.vector.scalar_tensor_tensor(out=dta[:], in0=dt[:], scalar=-1.0, in1=bcast(a[:].unsqueeze(1), [P, NT, DH]),
                                           op0=ALU.mult, op1=ALU.mult).then_inc(pre["dta"], 1)
            dve.wait_ge(pre["sums"], 1)
            sums = [k.ps[:, o, 0:NT * DH].rearrange("p (t c) -> p t c", t=NT) for o in range(3)]
            nc.vector.tensor_copy(cs[:, :, 0:HEADS], sums[0][:, :, 0:HEADS])
            nc.vector.tensor_copy(cs[:, :, HEADS:DH], sums[1][:, :, HEADS:DH])
            nc.vector.tensor_copy(etot[:], sums[2])
            dve.drain()
            nc.vector.tensor_tensor(wend[:], etot[:], cs[:], ALU.subtract)
            nc.vector.tensor_scalar(ncs[:], cs[:], -1.0, None, ALU.mult).then_inc(pre["cs"], 1)
            dve.wait_ge(pre["cs"], 1)
            dve.wait_ge(pre["ecs"], 1)
            nc.vector.tensor_tensor(wend[:], wend[:], dt[:], ALU.mult)
            nc.vector.memset(state[:], 0.0).then_inc(zero_state, 1)
            dve.drain()
            dve.sem_inc(pre["ready"], 1)
            heads = lambda t: t.rearrange("p (h e) -> p h e", h=HPG)

            def weigh_ends(i):
                d, c = steps[i]
                if i:
                    dve.wait_ge(s_full, i * GROUPS)
                nc.vector.tensor_tensor(xw[:].rearrange("p (h e) -> p h e", h=HEADS), xb[:, c, 0:DI].rearrange("p (h e) -> p h e", h=HEADS),
                                        bcast(wend[:, c, d * HEADS:(d + 1) * HEADS].unsqueeze(2), [P, HEADS, HD]), ALU.mult).then_inc(xw_ready, 1)
                if i == NT:
                    dve.wait_ge(s_read, i * GROUPS)
                    nc.vector.memset(state[:], 0.0).then_inc(zero_state, 1)
                    dve.drain()

            def mask(G):
                d = steps[G // GROUPS][0]
                dve.wait_ge(cb_full, G + 1)
                if G > AHEAD:
                    dve.wait_ge(weighed, 2 * (G - AHEAD))
                nc.vector.tensor_tensor(cbm[:, G % (AHEAD + 1), :], k.ps[:, 2, 0:P], k.tri[:, d, :], ALU.mult).then_inc(cb_masked, 1)

            def clamp(n):
                (d, c), g = steps[n // 2 // GROUPS], n // 2 % GROUPS
                dve.wait_ge(row_full, n + 1)
                if n >= 4:
                    dve.wait_ge(exped, n - 3)
                h = d * HEADS + g * HPG + (n % 2) * 4
                nc.vector.tensor_tensor(seg[:, n % 4, :].rearrange("p (r e) -> p r e", r=4),
                                        k.ps[:, n % 2, :].rearrange("p (r e) -> p r e", r=4),
                                        bcast(cs[:, c, h:h + 4].unsqueeze(2), [P, 4, P]), ALU.min).then_inc(clamped, 1)

            weigh_ends(0)
            for F in range(NG + AHEAD):
                G = F - AHEAD
                if F < NG:
                    mask(F)
                if G >= 0:
                    i, g = G // GROUPS, G % GROUPS
                    d, c = steps[i]
                    hs = slice(d * HEADS + g * HPG, d * HEADS + (g + 1) * HPG)
                    cols = slice(g * BANK, (g + 1) * BANK)
                    dve.wait_ge(off_full, G + 1)
                    nc.vector.tensor_tensor(heads(off[:]), heads(k.ps[:, 5, :]),
                                            bcast(ecs[:, c, hs].unsqueeze(2), [P, HPG, HD]), ALU.mult).then_inc(off_read, 1)
                    nc.vector.tensor_tensor(heads(state[:, cols]), heads(state[:, cols]),
                                            bcast(etot[:, c, hs].unsqueeze(2), [P, HPG, HD]), ALU.mult)
                    dve.drain()
                    if g == 0 and i < NT:
                        dve.wait_ge(pre["y0"], i + 1)
                    nc.vector.tensor_tensor(y[:, c, cols], y[:, c, cols], off[:], ALU.add)
                if F < NG:
                    clamp(2 * F)
                if G >= 0:
                    dve.wait_ge(s_full, G + 1)
                    nc.vector.tensor_tensor(state[:, cols], state[:, cols], k.ps[:, 6 + G % 2, :], ALU.add).then_inc(s_read, 1)
                if F < NG:
                    clamp(2 * F + 1)
                if G >= 0:
                    dve.wait_ge(y_full, G + 1)
                    dve.drain()
                    nc.vector.tensor_tensor(y[:, c, cols], y[:, c, cols], k.ps[:, 3 + G % 2, :], ALU.add).then_inc(y_read, 1)
                    if g == GROUPS - 1 and i + 1 < NS:
                        weigh_ends(i + 1)


def ssd_output_stage(k, y, src, dst):
    nc, ins = k.nc, k.ins
    with ExitStack() as ctx:
        sb = sbuf(ctx, nc)
        w = sb("so_w", [P, MX, D])
        ng = sb("so_ng", [P, MX])
        zt = sb("so_z", [P, 2, DI])
        junk = sb("so_junk", [P, DI])
        sq = sb("so_sq", [P, D])
        yT = sb("so_yT", [P, 2, MX, P])
        x = sb("so_x", [P, 2, D])
        gate = sb("so_gate", [P, 2, D])
        ss, sd, rs = sb("so_ss", [P, NT]), sb("so_sd", [P, NT]), sb("so_rs", [P, NT])
        w_in, small_in = [k.sem(f"so_w_in{q}") for q in range(4)], k.sem("so_small_in")
        ng_in = k.sem("so_ng_in")
        z_in = [k.sem(f"so_z_in{s}") for s in range(2)]
        x_in = [k.sem(f"so_x_in{s}") for s in range(2)]
        gated, squared, mean, root, inv = (k.sem("so_gated"), k.sem("so_squared"), k.sem("so_mean"), k.sem("so_root"), k.sem("so_inv"))
        turned, copied, full, added = k.sem("so_turned"), k.sem("so_copied"), k.sem("so_full"), k.sem("so_added")
        stored = [k.sem(f"so_stored{s}") for s in range(2)]
        block = ctx.enter_context(nc.Block())

        @block.sync
        def _(sp):
            def load_z(t):
                if t >= 2:
                    sp.wait_ge(gated, t - 1)
                sp.dma_start(zt[:, t % 2, :].rearrange("p (n c) -> p n c", n=4), k.z[:, t].rearrange("n p c -> p n c")).then_inc(z_in[t % 2], 16)

            def load_x(t):
                if t >= 2:
                    sp.wait_ge(stored[t % 2], 16 * (t // 2))
                sp.dma_start(x[:, t % 2, :], src[t]).then_inc(x_in[t % 2], 16)

            load_z(0)
            sp.dma_start(ng[:], ins["ssd_norm_g"]).then_inc(ng_in, 16)
            for q in range(4):
                sp.dma_start(w[:, 4 * q:4 * q + 4, :], ins["ssd_out_w"][:, 4 * q:4 * q + 4, :]).then_inc(w_in[q], 16)
                if q == 0:
                    load_z(1)
            load_x(0)
            load_x(1)
            for r, t in ((0, 0), (1, LAT)):
                sp.dma_start(gate[:, r, :], k.mods[0, t, 2 * D:3 * D].partition_broadcast(P)).then_inc(small_in, 16)
            for t in range(NT):
                if t + 2 < NT:
                    load_z(t + 2)
                sp.wait_ge(added, t + 1)
                sp.dma_start(dst[t], x[:, t % 2, :]).then_inc(stored[t % 2], 16)
                if t + 2 < NT:
                    load_x(t + 2)
            for s in range(2):
                sp.wait_ge(stored[s], 16 * NT // 2)

        @block.vector
        def _(dve):
            def gate_tile(t):
                dve.wait_ge(z_in[t % 2], 16 * (t // 2 + 1))
                nc.vector.tensor_tensor(y[:, t, :], y[:, t, :], zt[:, t % 2, :], ALU.mult).then_inc(gated, 1)

            def scale_turned(t):
                if t >= 2:
                    dve.wait_ge(full, t - 1)
                for q in range(4):
                    n = t * 4 + q
                    dve.wait_ge(turned, n + 1)
                    nc.vector.tensor_tensor(yT[:, t % 2, 4 * q:4 * q + 4, :], k.ps[:, n % 4, :].rearrange("p (m c) -> p m c", m=4),
                                            bcast(ng[:, 4 * q:4 * q + 4].unsqueeze(2), [P, 4, P]), ALU.mult).then_inc(copied, 1)

            gate_tile(0)
            dve.wait_ge(ng_in, 16)
            scale_turned(0)
            gate_tile(1)
            dve.wait_ge(small_in, 32)
            for t in range(NT):
                if t + 2 < NT:
                    gate_tile(t + 2)
                if t + 1 < NT:
                    scale_turned(t + 1)
                dve.wait_ge(squared, t + 1)
                nc.vector.tensor_scalar(sd[:, t:t + 1], ss[:, t:t + 1], 1.0 / DI, EPS, ALU.mult, ALU.add).then_inc(mean, 1)
                dve.wait_ge(root, t + 1)
                nc.vector.reciprocal(rs[:, t:t + 1], sd[:, t:t + 1])
                r = 0 if t < LAT else 1
                dve.wait_ge(full, t + 1)
                dve.drain()
                b = 4 + 2 * (t % 2)
                nc.vector.scalar_tensor_tensor(out=sq[:], in0=k.flat[:, b * BANK:(b + 2) * BANK], scalar=rs[:, t:t + 1], in1=gate[:, r, :],
                                               op0=ALU.mult, op1=ALU.mult)
                dve.wait_ge(x_in[t % 2], 16 * (t // 2 + 1))
                dve.drain()
                nc.vector.tensor_tensor(x[:, t % 2, :], x[:, t % 2, :], sq[:], ALU.add).then_inc(added, 1)

        @block.scalar
        def _(act):
            for t in range(NT):
                act.wait_ge(gated, t + 1)
                nc.scalar.activation(junk[:], y[:, t, :], ACT.Square, accum_out=ss[:, t:t + 1]).then_inc(squared, 1)
                act.wait_ge(mean, t + 1)
                nc.scalar.activation(sd[:, t:t + 1], sd[:, t:t + 1], ACT.Sqrt).then_inc(root, 1)

        @block.tensor
        def _(pe):
            def turn(t):
                pe.wait_ge(gated, t + 1)
                for q in range(4):
                    n = t * 4 + q
                    if n >= 4:
                        pe.wait_ge(copied, n - 3)
                    for m in range(4):
                        mm = nc.tensor.transpose(k.ps[:, n % 4, m * P:(m + 1) * P], y[:, t, (4 * q + m) * P:(4 * q + m + 1) * P], k.ident[:])
                    mm.then_inc(turned, 1)

            turn(0)
            for t in range(NT):
                if t + 1 < NT:
                    turn(t + 1)
                if t >= 2:
                    pe.wait_ge(added, t - 1)
                pe.wait_ge(copied, (t + 1) * 4)
                b = 4 + 2 * (t % 2)
                for m in range(MX):
                    if t == 0 and m % 4 == 0:
                        pe.wait_ge(w_in[m // 4], 16)
                    for n in range(2):
                        mm = nc.tensor.matmul(k.ps[:, b + n, :], yT[:, t % 2, m, :], w[:, m, n * BANK:(n + 1) * BANK], start=m == 0, stop=m == MX - 1)
                mm.then_inc(full, 1)


def peer_stage(k, layer, tiles, hT, wq, keys, src, dst):
    nc, ins = k.nc, k.ins
    E = TOPK
    HALF = E // 2
    with ExitStack() as ctx:
        sb = sbuf(ctx, nc)
        iota = sb("pe_iota", [P, TOPK])
        hTb = sb("pe_hTb", [P, KD, P])
        q, qT = sb("pe_q", [P, 2 * P]), sb("pe_qT", [P, 2, P])
        rest, crest = sb("pe_rest", [P, NKEYS]), sb("pe_crest", [P, TOPK * TOPK])
        top, topi, topf = sb("pe_top", [P, 2, TOPK]), sb("pe_topi", [P, 2, TOPK], U32), sb("pe_topf", [P, 2, TOPK])
        cand, best, pos = sb("pe_cand", [P, TOPK * TOPK]), sb("pe_best", [P, TOPK]), sb("pe_pos", [P, TOPK], U32)
        part, partf = sb("pe_part", [P, 2, TOPK], U32), sb("pe_partf", [P, 2, TOPK])
        hot, half, idf = sb("pe_hot", [P, 2, TOPK, TOPK]), sb("pe_half", [P, 2, TOPK]), sb("pe_idf", [P, TOPK])
        scores, shift, tot = sb("pe_scores", [P, PH, TOPK]), sb("pe_shift", [P, PH]), sb("pe_tot", [P, PH])
        ids, gates = sb("pe_ids", [P, NT * PH * TOPK], U32), sb("pe_gates", [P, NT * PH * TOPK])
        ring = sb("pe_ring", [P, SLOTS, 2 * D])
        idx = sb("pe_idx", [P, E], U32)
        gate = sb("pe_gate", [P, E])
        dot, act_out, weight = sb("pe_dot", [P, E]), sb("pe_act", [P, E]), sb("pe_weight", [P, E])
        hn, h = sb("pe_h_next", [P, D]), sb("pe_h", [P, D])
        diag = sb("pe_diag", [P, 2, P])
        acc, x, g2 = sb("pe_acc", [P, D]), sb("pe_x", [P, D]), sb("pe_g2", [P, D])

        iota_in, hTb_ready = k.sem("pe_iota_in"), k.sem("pe_hTb_ready")
        projected, q_read, q_turned, qT_ready = k.sem("pe_projected"), k.sem("pe_q_read"), k.sem("pe_q_turned"), k.sem("pe_qT_ready")
        scored, ranked, chosen = k.sem("pe_scored"), k.sem("pe_ranked"), k.sem("pe_chosen")
        shifted, exped, gated, gate_staged = k.sem("pe_shifted"), k.sem("pe_exped"), k.sem("pe_gated"), k.sem("pe_gate_staged")
        landed = [k.sem(f"pe_landed{s}") for s in range(SLOTS)]
        slot_free, staged = [k.sem("pe_slot_free_by_pe"), k.sem("pe_slot_free_by_dve")], k.sem("pe_staged")
        diag_ready, sum_full, sum_read = k.sem("pe_diag_ready"), k.sem("pe_sum_full"), k.sem("pe_sum_read")
        h_in, h_free, x_in, out_ready, stored = k.sem("pe_h_in"), k.sem("pe_h_free"), k.sem("pe_x_in"), k.sem("pe_out_ready"), k.sem("pe_stored")
        dotted, gelued, weighted = k.sem("pe_dotted"), k.sem("pe_gelued"), k.sem("pe_weighted")
        block = ctx.enter_context(nc.Block())
        row = lambda dram, b: dram[bass.ds(b, 1)].rearrange("o p n -> (o p) n")

        @block.sync
        def _(sp):
            def block_io(b, last):
                sp.dma_start(x[:], row(src, b)).then_inc(x_in, 16)
                sp.dma_start(g2[:], k.mods[layer, bass.ds(b, 1), 5 * D:6 * D].rearrange("o n -> (o n)").partition_broadcast(P)).then_inc(x_in, 16)
                if not last:
                    k.hold(sp, "sp", h_free, b + 1)
                    sp.dma_start(hn[:], row(k.h, b + 1)).then_inc(h_in, 16)
                k.hold(sp, "sp", out_ready, b + 1)
                sp.dma_start(row(dst, b), x[:]).then_inc(stored, 16)
                k.hold(sp, "sp", stored, (b + 1) * 16)

            sp.dma_start(iota[:], ins["iota"].partition_broadcast(P)).then_inc(iota_in, 16)
            sp.dma_start(hn[:], k.h[0]).then_inc(h_in, 16)
            with sp.Fori(0, tiles - 1) as b:
                block_io(b, False)
            block_io(tiles - 1, True)

        @block.gpsimd
        def _(pool):
            with pool.Fori(0, tiles * PH) as i:
                k.hold(pool, "pool", chosen, i + 1)
                for e in range(E):
                    k.hold(pool, "pool", slot_free[e % 2], i * HALF + e // 2 + 1)
                    if e % 8 == 0:
                        nc.gpsimd.tensor_copy(idx[:, e:e + 8], ids[:, bass.ds(i * E + e, 8)]).then_inc(staged, 1)
                        k.hold(pool, "pool", staged, i * 2 + e // 8 + 1)
                    pool.indirect_dma_start(out=ring[:, e % SLOTS, :], out_offset=None, in_=ins[f"peer_uv{layer}"],
                                            in_offset=bass.IndirectOffsetOnAxis(ap=idx[:, e:e + 1], axis=0)).then_inc(landed[e % SLOTS], 16)

        @block.tensor
        def _(pe):
            pe.sem_inc(q_read, 1)
            pe.sem_inc(qT_ready, 1)
            pe.sem_inc(ranked, 1)
            pe.sem_inc(sum_read, 1)
            pe.sem_inc(slot_free[0], SLOTS // 2)

            def project(u, head):
                k.hold(pe, "pe", q_read, u + 1)
                for kt in range(KD):
                    mm = nc.tensor.matmul(k.ps[:, 0, 0:2 * P], hTb[:, kt, :], wq[:, bass.ds(head * (KD * 2 * P) + kt * 2 * P, 2 * P)],
                                          start=kt == 0, stop=kt == KD - 1)
                mm.then_inc(projected, 1)

            def turn(u):
                k.hold(pe, "pe", q_read, u + 2)
                k.hold(pe, "pe", qT_ready, u + 1)
                for c in range(2):
                    mm = nc.tensor.transpose(k.ps[:, 1, c * P:(c + 1) * P], q[:, c * P:(c + 1) * P], k.ident[:])
                mm.then_inc(q_turned, 1)

            def score(u, head):
                k.hold(pe, "pe", qT_ready, u + 2)
                k.hold(pe, "pe", ranked, u + 1)
                for c in range(2):
                    mm = nc.tensor.matmul(k.ps[:, 2, c * P:(c + 1) * P], qT[:, c, :], keys[:, bass.ds(head * 2 * P + c * P, P)],
                                          start=True, stop=True)
                mm.then_inc(scored, 1)

            def add_expert(i, e):
                if e == 0:
                    k.hold(pe, "pe", sum_read, i + 1)
                k.hold(pe, "pe", diag_ready, i * HALF + e // 2 + 1)
                for n in range(2):
                    mm = nc.tensor.matmul(k.ps[:, 3 + n, :], diag[:, e // 2 % 2, :], ring[:, e % SLOTS, D + n * BANK:D + (n + 1) * BANK],
                                          start=e == 0, stop=e == E - 2)
                mm.then_inc(slot_free[0], 1)
                if e == E - 2:
                    k.hold(pe, "pe", slot_free[0], i * HALF + HALF + SLOTS // 2)
                    pe.sem_inc(sum_full, 1)

            k.hold(pe, "pe", hTb_ready, 1)
            with pe.Fori(0, PH) as head:
                project(head, head)
                turn(head)
                score(head, head)
            with pe.Fori(0, tiles - 1) as b:
                k.hold(pe, "pe", hTb_ready, b + 2)
                with pe.Fori(0, PH) as head:
                    i = b * PH + head
                    u = (b + 1) * PH + head
                    project(u, head)
                    for e in range(0, E, 2):
                        add_expert(i, e)
                        if e == 2:
                            turn(u)
                        if e == 4:
                            score(u, head)
            with pe.Fori(0, PH) as head:
                for e in range(0, E, 2):
                    add_expert(head + (tiles - 1) * PH, e)

        @block.scalar
        def _(act):
            def read_q(u):
                k.hold(act, "act", projected, u + 1)
                k.hold(act, "act", qT_ready, u + 1)
                nc.scalar.activation(q[:], k.ps[:, 0, 0:2 * P], ACT.Copy).then_inc(q_read, 1)

            def read_qT(u):
                k.hold(act, "act", q_turned, u + 1)
                nc.scalar.activation(qT[:], k.ps[:, 1, 0:2 * P].rearrange("p (c e) -> p c e", c=2), ACT.Copy).then_inc(qT_ready, 1)

            def take_hT(b):
                nc.scalar.activation(hTb[:], hT[:, :, bass.ds(b * P, P)], ACT.Copy).then_inc(hTb_ready, 1)

            def exp_scores(b):
                k.hold(act, "act", shifted, b + 1)
                nc.scalar.activation(scores[:], scores[:], ACT.Exp).then_inc(exped, 1)

            def experts(i, u):
                act.drain()
                nc.scalar.activation(gate[:], gates[:, bass.ds(i * E, E)], ACT.Copy).then_inc(gate_staged, 1)
                k.hold(act, "act", gate_staged, i + 1)
                for e in range(E):
                    n = i * E + e + 1
                    act.wait_ge(dotted, n)
                    nc.scalar.activation(act_out[:, e:e + 1], dot[:, e:e + 1], ACT.Gelu).then_inc(gelued, 1)
                    act.wait_ge(gelued, n)
                    nc.scalar.activation(weight[:, e:e + 1], act_out[:, e:e + 1], ACT.Copy, scale=gate[:, e:e + 1]).then_inc(weighted, 1)
                    if e % 2 == 0:
                        act.wait_ge(weighted, n)
                        k.hold(act, "act", slot_free[0], i * HALF + e // 2 + SLOTS // 2 - 1)
                        nc.scalar.activation(diag[:, e // 2 % 2, :], k.ident[:], ACT.Copy, scale=weight[:, e:e + 1]).then_inc(diag_ready, 1)
                    if u is not None and e == 3:
                        read_q(u)
                    if u is not None and e == 5:
                        read_qT(u)

            take_hT(0)
            with act.Fori(0, PH) as head:
                read_q(head)
                read_qT(head)
            exp_scores(0)
            with act.Fori(0, tiles - 1) as b:
                k.hold(act, "act", projected, (b + 1) * PH)
                take_hT(b + 1)
                k.hold(act, "act", gated, b + 1)
                with act.Fori(0, PH) as head:
                    experts(b * PH + head, (b + 1) * PH + head)
                exp_scores(b + 1)
            act.wait_ge(gated, tiles)
            with act.Fori(0, PH) as head:
                experts(head + (tiles - 1) * PH, None)

        @block.vector
        def _(dve):
            V = nc.vector
            dve.sem_inc(slot_free[1], SLOTS // 2)

            def top16(vals, left, out_v, out_i):
                V.max(out_v[:, 0:8], vals)
                dve.drain()
                V.max_index(out_i[:, 0:8], out_v[:, 0:8], vals)
                V.match_replace(left, out_v[:, 0:8], vals, NEG)
                dve.drain()
                V.max(out_v[:, 8:16], left)
                dve.drain()
                return V.max_index(out_i[:, 8:16], out_v[:, 8:16], left)

            def rank(u, c):
                if c == 0:
                    k.hold(dve, "dve", scored, u + 1)
                last = top16(k.ps[:, 2, c * P:(c + 1) * P], rest[:], top[:, c, :], topi[:, c, :])
                if c == 1:
                    last.then_inc(ranked, 1)

            def combine():
                V.tensor_copy(topf[:], topi[:])
                V.tensor_tensor(cand[:].rearrange("p (a b) -> p a b", a=TOPK), bcast(top[:, 0, :].unsqueeze(2), [P, TOPK, TOPK]),
                                bcast(top[:, 1, :].unsqueeze(1), [P, TOPK, TOPK]), ALU.add)
                dve.drain()
                top16(cand[:], crest[:], best[:], pos[:])
                dve.drain()

            def look_up():
                V.tensor_scalar(part[:, 0, :], pos[:], 4, None, ALU.logical_shift_right)
                V.tensor_scalar(part[:, 1, :], pos[:], 15, None, ALU.bitwise_and)
                dve.drain()
                V.tensor_copy(partf[:], part[:])
                dve.drain()
                V.tensor_tensor(hot[:], bcast(partf[:].unsqueeze(3), [P, 2, TOPK, TOPK]),
                                bcast(iota[:].unsqueeze(1).unsqueeze(1), [P, 2, TOPK, TOPK]), ALU.is_equal)
                dve.drain()
                V.tensor_tensor(hot[:], hot[:], bcast(topf[:].unsqueeze(2), [P, 2, TOPK, TOPK]), ALU.mult)
                dve.drain()

            def choose(u, head):
                V.tensor_reduce(half[:], hot[:], AX.X, ALU.add)
                V.tensor_copy(scores[:].rearrange("p h e -> p (h e)")[:, bass.ds(head * TOPK, TOPK)], best[:])
                dve.drain()
                V.scalar_tensor_tensor(out=idf[:], in0=half[:, 0, :], scalar=float(NKEYS), in1=half[:, 1, :], op0=ALU.mult, op1=ALU.add)
                dve.drain()
                V.tensor_copy(ids[:, bass.ds(u * TOPK, TOPK)], idf[:]).then_inc(chosen, 1)

            def shift_scores():
                dve.drain()
                V.tensor_copy(shift[:], scores[:, :, 0])
                dve.drain()
                V.tensor_tensor(scores[:], scores[:], bcast(shift[:].unsqueeze(2), [P, PH, TOPK]), ALU.subtract).then_inc(shifted, 1)

            def normalize(b):
                k.hold(dve, "dve", exped, b + 1)
                V.tensor_reduce(tot[:], scores[:], AX.X, ALU.add)
                dve.drain()
                V.reciprocal(tot[:], tot[:])
                dve.drain()
                V.tensor_tensor(scores[:], scores[:], bcast(tot[:].unsqueeze(2), [P, PH, TOPK]), ALU.mult)
                dve.drain()
                V.tensor_copy(gates[:, bass.ds(b * PH * TOPK, PH * TOPK)], scores[:].rearrange("p h e -> p (h e)")).then_inc(gated, 1)

            def add_expert(i, e):
                dve.wait_ge(slot_free[1], i * HALF + e // 2 + SLOTS // 2)
                dve.wait_ge(weighted, i * E + e + 1)
                V.scalar_tensor_tensor(out=acc[:], in0=ring[:, e % SLOTS, D:2 * D], scalar=weight[:, e:e + 1], in1=acc[:],
                                       op0=ALU.mult, op1=ALU.add).then_inc(slot_free[1], 1)

            def add_sum(i):
                dve.drain()
                k.hold(dve, "dve", sum_full, i + 1)
                V.tensor_tensor(acc[:], acc[:], k.flat[:, 3 * BANK:5 * BANK], ALU.add).then_inc(sum_read, 1)
                dve.drain()

            def start_block(b):
                k.hold(dve, "dve", h_in, (b + 1) * 16)
                V.tensor_copy(h[:], hn[:])
                V.memset(acc[:], 0.0)
                dve.drain()
                dve.sem_inc(h_free, 1)

            def end_block(b):
                dve.drain()
                k.hold(dve, "dve", x_in, (b + 1) * 32)
                V.tensor_tensor(acc[:], acc[:], g2[:], ALU.mult)
                dve.drain()
                V.tensor_tensor(x[:], acc[:], x[:], ALU.add).then_inc(out_ready, 1)
                dve.drain()

            def experts(i, u, head):
                for e in range(E):
                    dve.wait_ge(landed[e % SLOTS], i * 32 + 16 * (e // SLOTS + 1))
                    V.tensor_tensor_reduce(out=ring[:, e % SLOTS, 0:D], in0=ring[:, e % SLOTS, 0:D], in1=h[:], scale=1.0, scalar=0.0,
                                           op0=ALU.mult, op1=ALU.add, accum_out=dot[:, e:e + 1]).then_inc(dotted, 1)
                    if e and e % 2 == 0:
                        add_expert(i, e - 1)
                    if u is None:
                        continue
                    if e == 7:
                        rank(u, 0)
                    if e == 9:
                        rank(u, 1)
                        dve.drain()
                    if e == 11:
                        combine()
                    if e == 13:
                        look_up()
                    if e == 15:
                        choose(u, head)
                add_expert(i, E - 1)
                add_sum(i)

            dve.wait_ge(iota_in, 16)
            with dve.Fori(0, PH) as head:
                rank(head, 0)
                rank(head, 1)
                dve.drain()
                combine()
                look_up()
                choose(head, head)
                dve.drain()
            shift_scores()
            normalize(0)
            with dve.Fori(0, tiles - 1) as b:
                start_block(b)
                with dve.Fori(0, PH) as head:
                    experts(b * PH + head, (b + 1) * PH + head, head)
                shift_scores()
                end_block(b)
                normalize(b + 1)
            start_block(tiles - 1)
            with dve.Fori(0, PH) as head:
                experts(head + (tiles - 1) * PH, None, None)
            end_block(tiles - 1)


def attention_project_stage(k, hT, qT, kT, v):
    nc, ins = k.nc, k.ins
    RW = 4
    with ExitStack() as ctx:
        sb = sbuf(ctx, nc)
        w = sb("ap_w", [P, RW, KD * P])
        wv = sb("ap_wv", [P, 2, KD * BANK])
        rope = sb("ap_rope", [P, 2, TL])
        rot = sb("ap_rot", [P, P])
        raw = sb("ap_raw", [P, 2, TL])
        rs = sb("ap_rs", [P, 2, TL])
        w_in = [k.sem(f"ap_w_in{s}") for s in range(RW)]
        wv_in, small_in = k.sem("ap_wv_in"), k.sem("ap_small_in")
        projected, raw_ready, rotated, done = k.sem("ap_projected"), k.sem("ap_raw_ready"), k.sem("ap_rotated"), k.sem("ap_done")
        v_full, v_read = k.sem("ap_v_full"), k.sem("ap_v_read")
        block = ctx.enter_context(nc.Block())
        NM = 2 * AH

        @block.sync
        def _(sp):
            for m in range(NM):
                if m >= RW:
                    sp.wait_ge(projected, m - RW + 1)
                sp.dma_start(w[:, m % RW, :], ins["w_qk"][m]).then_inc(w_in[m % RW], 16)
                if m == 0:
                    sp.dma_start(rope[:], ins["rope"]).then_inc(small_in, 16)
                    sp.dma_start(rot[:], ins["rot"]).then_inc(small_in, 16)
            for n in range(2):
                sp.dma_start(wv[:, n, :], ins["w_v"][n]).then_inc(wv_in, 16)

        @block.tensor
        def _(pe):
            def rotate(m):
                pe.wait_ge(raw_ready, m + 1)
                if m >= 2:
                    pe.wait_ge(done, m - 1)
                nc.tensor.matmul(k.ps[:, 4 + m % 2, :], rot[:], raw[:, m % 2, :], start=True, stop=True).then_inc(rotated, 1)

            pe.wait_ge(small_in, 32)
            for m in range(NM + 1):
                if m < NM:
                    pe.wait_ge(w_in[m % RW], 16 * (m // RW + 1))
                    if m >= 2:
                        pe.wait_ge(raw_ready, m - 1)
                    for kt in range(KD):
                        mm = nc.tensor.matmul(k.ps[:, 2 * (m % 2), :], w[:, m % RW, kt * P:(kt + 1) * P], hT[:, kt, 0:TL],
                                              start=kt == 0, stop=kt == KD - 1)
                        if m >= AH:
                            mm = nc.tensor.matmul(k.ps[:, 2 * (m % 2) + 1, 0:CTX * P], w[:, m % RW, kt * P:(kt + 1) * P], hT[:, kt, TL:T],
                                                  start=kt == 0, stop=kt == KD - 1)
                    mm.then_inc(projected, 1)
                if m:
                    rotate(m - 1)
            pe.wait_ge(wv_in, 32)
            for n in range(2):
                for t in range(NT):
                    i = n * NT + t
                    if i >= 2:
                        pe.wait_ge(v_read, i - 1)
                    for kt in range(KD):
                        mm = nc.tensor.matmul(k.ps[:, 6 + i % 2, :], hT[:, kt, t * P:(t + 1) * P], wv[:, n, kt * BANK:(kt + 1) * BANK],
                                              start=kt == 0, stop=kt == KD - 1)
                    mm.then_inc(v_full, 1)

        @block.scalar
        def _(act):
            for m in range(NM):
                act.wait_ge(projected, m + 1)
                if m >= 2:
                    act.wait_ge(done, m - 1)
                if m >= AH:
                    nc.scalar.activation(kT[:, m - AH, TL:T], k.ps[:, 2 * (m % 2) + 1, 0:CTX * P], ACT.Copy)
                nc.scalar.activation(raw[:, m % 2, :], k.ps[:, 2 * (m % 2), :], ACT.Copy, scale=0.125 if m < AH else 1.0).then_inc(raw_ready, 1)
            for n in range(2):
                for t in range(NT):
                    i = n * NT + t
                    act.wait_ge(v_full, i + 1)
                    nc.scalar.activation(v[:, t, n * BANK:(n + 1) * BANK], k.ps[:, 6 + i % 2, :], ACT.Copy).then_inc(v_read, 1)

        @block.vector
        def _(dve):
            dve.wait_ge(small_in, 32)
            for m in range(NM):
                dst = qT[:, m, :] if m < AH else kT[:, m - AH, 0:TL]
                dve.wait_ge(rotated, m + 1)
                nc.vector.tensor_tensor(rs[:, m % 2, :], k.ps[:, 4 + m % 2, :], rope[:, 1, :], ALU.mult)
                nc.vector.tensor_tensor(dst, raw[:, m % 2, :], rope[:, 0, :], ALU.mult)
                dve.drain()
                nc.vector.tensor_tensor(dst, dst, rs[:, m % 2, :], ALU.add).then_inc(done, 1)


def attend_stage(k, qT, kT, v, o):
    nc, ins = k.nc, k.ins
    with ExitStack() as ctx:
        sb = sbuf(ctx, nc)
        lam = sb("at_lam", [P, 2, P])
        ls = sb("at_ls", [P, 2])
        nl = sb("at_nl", [P, 1])
        p = sb("at_p", [P, 2, 2, T])
        wT = sb("at_wT", [P, 2, T])
        nmax, tot, inv = sb("at_nmax", [P, 2, 2]), sb("at_tot", [P, 2, 2]), sb("at_inv", [P, 2, 2])
        lam_in, lam_sum, lam_exp = k.sem("at_lam_in"), k.sem("at_lam_sum"), k.sem("at_lam_exp")
        scored, maxed, exped, combined = k.sem("at_scored"), k.sem("at_maxed"), k.sem("at_exped"), k.sem("at_combined")
        turned, copied, full, read = k.sem("at_turned"), k.sem("at_copied"), k.sem("at_full"), k.sem("at_read")
        block = ctx.enter_context(nc.Block())
        N = LAT * AH

        @block.sync
        def _(sp):
            sp.dma_start(lam[:, 0, :], ins["lambda_q"].partition_broadcast(P)).then_inc(lam_in, 16)
            sp.dma_start(lam[:, 1, :], ins["lambda_k"].partition_broadcast(P)).then_inc(lam_in, 16)

        @block.tensor
        def _(pe):
            def score(n):
                t, h = n // AH, n % AH
                rows = slice(64 * (h % 2), 64 * (h % 2) + 64)
                for mp in range(2):
                    if n >= 1:
                        pe.wait_ge(exped, 2 * (n - 1) + mp + 1)
                    m = mp * 4 + h // 2
                    for o_, a, c in ((0, 0, TL), (BANK, TL, CTX * P)):
                        mm = nc.tensor.matmul(k.flat[:, mp * 2 * BANK + o_:mp * 2 * BANK + o_ + c], qT[rows, m, t * P:(t + 1) * P],
                                              kT[rows, m, a:a + c], start=True, stop=True)
                    mm.then_inc(scored, 1)

            def turn(n):
                pe.wait_ge(combined, n + 1)
                if n >= 1:
                    pe.wait_ge(copied, n)
                for t in range(NT):
                    mm = nc.tensor.transpose(k.flat[:, 4 * BANK + t * P:4 * BANK + (t + 1) * P], p[:, n % 2, 0, t * P:(t + 1) * P], k.ident[:])
                mm.then_inc(turned, 1)

            def values(n):
                h = n % AH
                pe.wait_ge(copied, n + 1)
                if n >= 2:
                    pe.wait_ge(read, n - 1)
                for t in range(NT):
                    mm = nc.tensor.matmul(k.ps[:, 6 + n % 2, 0:P], wT[:, n % 2, t * P:(t + 1) * P], v[:, t, h * AV:(h + 1) * AV],
                                          start=t == 0, stop=t == NT - 1)
                mm.then_inc(full, 1)

            for n in range(N + 2):
                if n < N:
                    score(n)
                if n >= 2:
                    values(n - 2)
                if 1 <= n <= N:
                    turn(n - 1)

        @block.scalar
        def _(act):
            act.wait_ge(lam_sum, 1)
            nc.scalar.activation(ls[:], ls[:], ACT.Exp).then_inc(lam_exp, 1)

            def tail(n):
                act.wait_ge(turned, n + 1)
                if n >= 2:
                    act.wait_ge(full, n - 1)
                nc.scalar.activation(wT[:, n % 2, :], k.flat[:, 4 * BANK:4 * BANK + T], ACT.Copy).then_inc(copied, 1)

            def read_out(n):
                act.wait_ge(full, n + 1)
                nc.scalar.activation(o[:, n // AH, (n % AH) * AV:(n % AH + 1) * AV], k.ps[:, 6 + n % 2, 0:P], ACT.Copy).then_inc(read, 1)

            for n in range(N + 2):
                if n < N:
                    if n >= 2:
                        act.wait_ge(turned, n - 1)
                    for mp in range(2):
                        act.wait_ge(maxed, 2 * n + mp + 1)
                        nc.scalar.activation(p[:, n % 2, mp, :], k.flat[:, mp * 2 * BANK:mp * 2 * BANK + T], ACT.Exp,
                                                    bias=nmax[:, n % 2, mp:mp + 1], accum_out=tot[:, n % 2, mp:mp + 1]).then_inc(exped, 1)
                if n >= 2:
                    read_out(n - 2)
                if 1 <= n <= N:
                    tail(n - 1)

        @block.vector
        def _(dve):
            V = nc.vector
            dve.wait_ge(lam_in, 32)
            V.tensor_tensor(lam[:, 0, :], lam[:, 0, :], lam[:, 1, :], ALU.mult)
            dve.drain()
            V.tensor_reduce(ls[:], lam[:, 0, :].rearrange("p (a b) -> p a b", a=2), AX.X, ALU.add).then_inc(lam_sum, 1)
            dve.wait_ge(lam_exp, 1)
            V.tensor_tensor(nl[:], ls[:, 1:2], ls[:, 0:1], ALU.subtract)
            dve.drain()
            V.tensor_scalar(nl[:], nl[:], -LAMBDA_INIT, None, ALU.add)
            dve.drain()

            def combine(n):
                s = n % 2
                dve.wait_ge(exped, 2 * n + 2)
                V.reciprocal(inv[:, s, :], tot[:, s, :])
                dve.drain()
                V.tensor_tensor(inv[:, s, 1:2], inv[:, s, 1:2], nl[:], ALU.mult)
                V.tensor_scalar(p[:, s, 0, :], p[:, s, 0, :], inv[:, s, 0:1], None, ALU.mult)
                dve.drain()
                V.scalar_tensor_tensor(out=p[:, s, 0, :], in0=p[:, s, 1, :], scalar=inv[:, s, 1:2], in1=p[:, s, 0, :],
                                       op0=ALU.mult, op1=ALU.add).then_inc(combined, 1)

            for n in range(N + 1):
                if n:
                    combine(n - 1)
                if n < N:
                    for mp in range(2):
                        dve.wait_ge(scored, 2 * n + mp + 1)
                        V.tensor_reduce(nmax[:, n % 2, mp:mp + 1], k.flat[:, mp * 2 * BANK:mp * 2 * BANK + T], AX.X, ALU.max,
                                        negate=True).then_inc(maxed, 1)


def attention_output_stage(k, o, src, dst):
    nc, ins = k.nc, k.ins
    with ExitStack() as ctx:
        sb = sbuf(ctx, nc)
        w = sb("ao_w", [P, AH, D])
        sg = sb("ao_sg", [P, 1])
        gate = sb("ao_gate", [P, D])
        x = sb("ao_x", [P, LAT, D])
        sq = sb("ao_sq", [P, D])
        ss = sb("ao_ss", [P, LAT, AH])
        oT = sb("ao_oT", [P, 2, AH, P])
        w_in, small_in, x_in = k.sem("ao_w_in"), k.sem("ao_small_in"), k.sem("ao_x_in")
        mean, root, normed, turned, copied = k.sem("ao_mean"), k.sem("ao_root"), k.sem("ao_normed"), k.sem("ao_turned"), k.sem("ao_copied")
        full, added, stored, scaled = k.sem("ao_full"), k.sem("ao_added"), k.sem("ao_stored"), k.sem("ao_scaled")
        block = ctx.enter_context(nc.Block())
        heads = lambda a: a.rearrange("p (h e) -> p h e", h=AH)

        @block.sync
        def _(sp):
            sp.dma_start(sg[:], ins["subln_g"]).then_inc(small_in, 16)
            sp.dma_start(gate[:], k.mods[1, 0, 2 * D:3 * D].partition_broadcast(P)).then_inc(small_in, 16)
            sp.dma_start(w[:], ins["attn_out_w"]).then_inc(w_in, 16)
            for t in range(LAT):
                sp.dma_start(x[:, t, :], src[t]).then_inc(x_in, 16)
            for t in range(LAT):
                sp.wait_ge(added, t + 1)
                sp.dma_start(dst[t], x[:, t, :]).then_inc(stored, 16)
            sp.wait_ge(stored, 16 * LAT)

        @block.scalar
        def _(act):
            def take_root(t):
                act.wait_ge(mean, t + 1)
                nc.scalar.activation(ss[:, t, :], ss[:, t, :], ACT.Sqrt).then_inc(root, 1)

            take_root(0)
            act.wait_ge(scaled, 1)
            for t in range(LAT):
                if t + 1 < LAT:
                    take_root(t + 1)
                if t >= 2:
                    act.wait_ge(full, t - 1)
                for q in range(2):
                    n = 2 * t + q
                    act.wait_ge(turned, n + 1)
                    nc.scalar.activation(oT[:, t % 2, 4 * q:4 * q + 4, :], k.ps[:, n % 4, :].rearrange("p (h e) -> p h e", h=4), ACT.Copy,
                                         scale=sg[:, 0:1]).then_inc(copied, 1)

        @block.vector
        def _(dve):
            V = nc.vector

            def add_out(t):
                b = 4 + 2 * (t % 2)
                dve.wait_ge(full, t + 1)
                dve.drain()
                V.tensor_tensor(sq[:], k.flat[:, b * BANK:(b + 2) * BANK], gate[:], ALU.mult)
                dve.drain()
                V.tensor_tensor(x[:, t, :], x[:, t, :], sq[:], ALU.add).then_inc(added, 1)

            for t in range(LAT):
                V.tensor_tensor(sq[:], o[:, t, :], o[:, t, :], ALU.mult)
                dve.drain()
                V.tensor_reduce(ss[:, t, :], heads(sq[:]), AX.X, ALU.add)
                dve.drain()
                V.tensor_scalar(ss[:, t, :], ss[:, t, :], 1.0 / AV, EPS, ALU.mult, ALU.add).then_inc(mean, 1)
                if t == 0:
                    dve.wait_ge(small_in, 32)
                    V.tensor_scalar(sg[:], sg[:], 1.0 - LAMBDA_INIT, None, ALU.mult).then_inc(scaled, 1)
                dve.wait_ge(root, t + 1)
                V.reciprocal(ss[:, t, :], ss[:, t, :])
                dve.drain()
                V.tensor_tensor(heads(o[:, t, :]), heads(o[:, t, :]), bcast(ss[:, t, :].unsqueeze(2), [P, AH, AV]), ALU.mult).then_inc(normed, 1)
            dve.wait_ge(x_in, 16 * LAT)
            for t in range(LAT):
                add_out(t)

        @block.tensor
        def _(pe):
            def turn(t):
                pe.wait_ge(normed, t + 1)
                for q in range(2):
                    n = 2 * t + q
                    if n >= 4:
                        pe.wait_ge(copied, n - 3)
                    for j in range(4):
                        h = 4 * q + j
                        mm = nc.tensor.transpose(k.ps[:, n % 4, j * P:(j + 1) * P], o[:, t, h * AV:(h + 1) * AV], k.ident[:])
                    mm.then_inc(turned, 1)

            turn(0)
            for t in range(LAT):
                if t + 1 < LAT:
                    turn(t + 1)
                if t == 0:
                    pe.wait_ge(w_in, 16)
                if t >= 2:
                    pe.wait_ge(added, t - 1)
                pe.wait_ge(copied, 2 * (t + 1))
                b = 4 + 2 * (t % 2)
                for n in range(2):
                    for h in range(AH):
                        mm = nc.tensor.matmul(k.ps[:, b + n, :], oT[:, t % 2, h, :], w[:, h, n * BANK:(n + 1) * BANK], start=h == 0, stop=h == AH - 1)
                mm.then_inc(full, 1)


def final_stage(k, src, out):
    nc, ins = k.nc, k.ins
    with ExitStack() as ctx:
        sb = sbuf(ctx, nc)
        x = sb("fi_x", [P, LAT, D])
        g = sb("fi_g", [P, D])
        sq = sb("fi_sq", [P, D])
        ss = sb("fi_ss", [P, LAT])
        g_in, squared, mean, root, ready, stored = (k.sem("fi_g_in"), k.sem("fi_squared"), k.sem("fi_mean"), k.sem("fi_root"),
                                                   k.sem("fi_ready"), k.sem("fi_stored"))
        x_in = [k.sem(f"fi_x_in{t}") for t in range(LAT)]
        block = ctx.enter_context(nc.Block())

        @block.sync
        def _(sp):
            for t in range(LAT):
                sp.dma_start(x[:, t, :], src[t]).then_inc(x_in[t], 16)
            sp.dma_start(g[:], ins["final_norm_g"].partition_broadcast(P)).then_inc(g_in, 16)
            for t in range(LAT):
                sp.wait_ge(ready, t + 1)
                sp.dma_start(out[0, t * P:(t + 1) * P, :], x[:, t, :]).then_inc(stored, 16)
            sp.wait_ge(stored, 16 * LAT)

        @block.scalar
        def _(act):
            for t in range(LAT):
                act.wait_ge(x_in[t], 16)
                if t:
                    act.wait_ge(squared, t)
                nc.scalar.activation(sq[:], x[:, t, :], ACT.Square, accum_out=ss[:, t:t + 1]).then_inc(squared, 1)
            act.wait_ge(mean, 1)
            nc.scalar.activation(ss[:], ss[:], ACT.Sqrt).then_inc(root, 1)

        @block.vector
        def _(dve):
            dve.wait_ge(squared, LAT)
            nc.vector.tensor_scalar(ss[:], ss[:], 1.0 / D, EPS, ALU.mult, ALU.add).then_inc(mean, 1)
            dve.wait_ge(root, 1)
            nc.vector.reciprocal(ss[:], ss[:])
            dve.wait_ge(g_in, 16)
            dve.drain()
            for t in range(LAT):
                nc.vector.scalar_tensor_tensor(out=x[:, t, :], in0=x[:, t, :], scalar=ss[:, t:t + 1], in1=g[:],
                                               op0=ALU.mult, op1=ALU.mult).then_inc(ready, 1)


def build(nc, ins, out, debug=False):
    with ExitStack() as top:
        k = Core(nc, top, ins, debug)
        sb = sbuf(top, nc)
        ident, tri, ones = sb("ident", [P, P]), sb("tri", [P, 2, P]), sb("ones", [P, P])
        k.ident, k.tri, k.ones = ident, tri, ones
        const_in = k.sem("const_in")
        with nc.Block() as block:
            @block.sync
            def _(sp):
                sp.dma_start(ident[:], ins["ident"]).then_inc(const_in, 16)
                sp.dma_start(tri[:], ins["tri"]).then_inc(const_in, 16)
                sp.dma_start(ones[:], ins["ones"]).then_inc(const_in, 16)
                sp.wait_ge(const_in, 48)
        k.end_stage()
        modulation_stage(k)
        k.end_stage()
        x1, x2, x3, x4 = k.xs
        with ExitStack() as ctx:
            wide = sbuf(ctx, nc)("y", [P, NT, DI])
            flat = wide[:].rearrange("p t c -> p (t c)")
            hT = flat[:, 0:KD * T].rearrange("p (k c) -> p k c", k=KD)
            w = flat[:, KD * T:KD * T + 4 * KD * P].rearrange("p (s c) -> p s c", s=4)
            norm_stage(k, ins["x_all"], 0, ins["norm_mix_g"][0], 0, 1, NT, hT, False)
            k.end_stage()
            with ExitStack() as scan:
                s2 = sbuf(scan, nc)
                xb, bct, dt = s2("xb", [P, NT, DI + MB * P]), s2("bct", [P, 2 * MB, T]), s2("dt", [P, NT, DH])
                ssd_project_stage(k, hT, w, xb, bct, dt)
                k.end_stage()
                ssd_scan_stage(k, xb, bct, dt, wide)
                k.end_stage()
            ssd_output_stage(k, wide, ins["x_all"], x1)
            k.end_stage()
        for layer in range(2):
            tiles = NT if layer == 0 else LAT
            src, dst = (x1, x2) if layer == 0 else (x3, x4)
            if layer == 1:
                with ExitStack() as ctx:
                    s2 = sbuf(ctx, nc)
                    o, qT, kT, v = s2("o", [P, LAT, D]), s2("qT", [P, AH, TL]), s2("kT", [P, AH, T]), s2("v", [P, NT, D])
                    with ExitStack() as c2:
                        hT = sbuf(c2, nc)("hT_a", [P, KD, T])
                        norm_stage(k, x2, 1, ins["norm_mix_g"][1], 0, 1, NT, hT, False)
                        k.end_stage()
                        attention_project_stage(k, hT, qT, kT, v)
                        k.end_stage()
                    attend_stage(k, qT, kT, v, o)
                    k.end_stage()
                    attention_output_stage(k, o, x2, x3)
                    k.end_stage()
            with ExitStack() as ctx:
                s2 = sbuf(ctx, nc)
                hT, keys = s2(f"hT_p{layer}", [P, KD, T]), s2(f"keys{layer}", [P, HC * NKEYS])
                wq = s2(f"wq{layer}", [P, PH * KD * 2 * P])
                ahead = [(wq[:], ins["peer_q_w"][layer]), (keys[:], ins["peer_keys"][layer])]
                norm_stage(k, src, layer, ins["norm_ffn_g"][layer], 3, 4, tiles, hT, True, ahead)
                k.end_stage()
                peer_stage(k, layer, tiles, hT, wq, keys, src, dst)
                k.end_stage()
        final_stage(k, x4, out)
        k.end_stage()


def lay_out(inputs):
    f = lambda n: np.asarray(inputs[n])
    cut = lambda w, n: np.ascontiguousarray(w.reshape(w.shape[0] // P, P, w.shape[1] // n, n).transpose(2, 1, 0, 3)).reshape(
        w.shape[1] // n, P, -1)
    cols = lambda v: np.ascontiguousarray(v.reshape(-1, P).T)
    a = {}
    a["x_all"] = np.concatenate([f("x")[0], f("ctx")[0]]).reshape(NT, P, D)
    a["c_cols"] = np.ascontiguousarray(np.stack([f("c")[0], f("c_ctx")]).reshape(2, KD, P).transpose(2, 1, 0))
    a["ada_w"] = np.concatenate([cut(f("ada_w")[l], BANK) for l in range(2)])
    a["ada_b"] = f("ada_b").reshape(1, -1)
    in_w = f("ssd_in_w")[0]
    a["w_z"] = cut(in_w[:, 0:DI], BANK)
    a["w_xbc"] = cut(in_w[:, DI:2 * DI + 2 * MB * P], P)
    a["w_dt"] = cut(in_w[:, 2 * DI + 2 * MB * P:], DH)[0]
    a["conv_w"] = np.ascontiguousarray(f("ssd_conv_w")[0].reshape(5, -1, P).transpose(2, 1, 0))
    a["conv_b"] = cols(f("ssd_conv_b")[0])
    a["dt_bias"], a["a_log"], a["ssd_d"] = (f(n)[0].reshape(-1) for n in ("ssd_dt_bias", "ssd_a_log", "ssd_d"))
    a["ssd_norm_g"] = cols(f("ssd_norm_g")[0])
    a["ssd_out_w"] = np.ascontiguousarray(f("ssd_out_w")[0].reshape(MX, P, D).transpose(1, 0, 2))
    a["norm_mix_g"], a["norm_ffn_g"], a["final_norm_g"] = f("norm_mix_g"), f("norm_ffn_g"), f("final_norm_g")
    qkv = f("attn_qkv_w")[0]
    a["w_qk"], a["w_v"] = cut(qkv[:, 0:2 * D], P), cut(qkv[:, 2 * D:], BANK)
    a["lambda_q"], a["lambda_k"] = f("attn_lambda_q")[0].reshape(-1), f("attn_lambda_k")[0].reshape(-1)
    a["subln_g"] = f("attn_subln_g")[0].reshape(P, 1)
    a["attn_out_w"] = np.ascontiguousarray(f("attn_out_w")[0].reshape(AH, P, D).transpose(1, 0, 2))
    a["peer_q_w"] = np.ascontiguousarray(f("peer_q_w").reshape(2, KD, P, PH, 2 * P).transpose(0, 2, 3, 1, 4)).reshape(2, P, -1)
    a["peer_keys"] = np.ascontiguousarray(f("peer_keys").reshape(2, HC, NKEYS, P).transpose(0, 3, 1, 2)).reshape(2, P, -1)
    for l in range(2):
        a[f"peer_uv{l}"] = np.concatenate([f("peer_u")[l], f("peer_v")[l]], axis=1)
    j, i = np.arange(P)[:, None], np.arange(P)[None, :]
    a["ident"] = np.eye(P, dtype=np.float32)
    a["ones"] = np.ones((P, P), np.float32)
    a["tri"] = np.stack([j <= i, j >= i], axis=1).astype(np.float32)
    a["iota"] = np.arange(TOPK, dtype=np.float32)
    tok = np.arange(TL)
    freq = np.float32(10000.0) ** (-np.arange(0, 32, 2, dtype=np.float32) / np.float32(32))
    row, col = (tok // 64).astype(np.float32)[:, None] * freq, (tok % 64).astype(np.float32)[:, None] * freq
    ang = np.concatenate([row, row, col, col], axis=1).astype(np.float32)
    ang = np.concatenate([ang, ang], axis=1).T
    a["rope"] = np.ascontiguousarray(np.stack([np.cos(ang), np.sin(ang)], axis=1)).astype(np.float32)
    rot = np.zeros((P, P), np.float32)
    for c in range(P):
        if c % 32 < 16:
            rot[c + 16, c] = -1.0
        else:
            rot[c - 16, c] = 1.0
    a["rot"] = rot
    return a


def kernel(**inputs):
    import concourse.bacc as bacc
    from concourse.bass_utils import run_bass_kernel_spmd as run

    nc = bacc.Bacc("TRN2", target_bir_lowering=False, num_devices=1)
    arrays = lay_out(inputs)
    ins = {n: nc.dram_tensor(f"in_{n}", a.shape, mybir.dt.from_np(a.dtype), kind="ExternalInput").ap() for n, a in arrays.items()}
    out = nc.dram_tensor("out", (1, TL, D), F32, kind="ExternalOutput").ap()
    build(nc, ins, out)
    r = run(nc, [{f"in_{n}": a for n, a in arrays.items()}], core_ids=[0])
    return r.results[0]["out"]
```
